# Optimizing a Trainium2 kernel written in Bass

```python
import math
import jax, jax.numpy as jnp
from jax import lax
import numpy as np

D_MODEL = 1024
BATCH = 1
SEQ = 256
DEPTH = 1

CTX_LEN = 256
GRID_W = 64
EPS = 1e-6

A_CHUNK = 128
A_GROUPS = 8
A_WIDTH = D_MODEL
A_GROUP_DIM = A_WIDTH // A_GROUPS
ROWS_PER_CHUNK = A_CHUNK // GRID_W

B_HEADS = 8
B_HEAD_DIM = 128
B_WIDTH = B_HEADS * B_HEAD_DIM
B_CONV = 5
B_CHUNK = 64

N_EXPERTS = 16
N_GROUPS = 4
EXPERTS_PER_GROUP = N_EXPERTS // N_GROUPS
TOP_K = 2
D_EXPERT = 512

IN_COLS = 2 * A_WIDTH + 4 * B_WIDTH + 4 * B_HEADS + 2 * D_MODEL
IN_SPLITS = (A_WIDTH, 2 * A_WIDTH, 2 * A_WIDTH + 3 * B_WIDTH, 2 * A_WIDTH + 4 * B_WIDTH,
             2 * A_WIDTH + 4 * B_WIDTH + 4 * B_HEADS, 2 * A_WIDTH + 4 * B_WIDTH + 4 * B_HEADS + D_MODEL)

kernel_name = 'hybrid_sgu_gdn_moe_dit_block'

def rmsnorm(x, gain):
    xf = x.astype(jnp.float32)
    xf = xf * lax.rsqrt(jnp.mean(jnp.square(xf), axis=-1, keepdims=True) + EPS)
    return (xf * gain.astype(jnp.float32)).astype(x.dtype)

def layernorm(x, gain):
    xf = x.astype(jnp.float32)
    mu = jnp.mean(xf, axis=-1, keepdims=True)
    var = jnp.mean(jnp.square(xf - mu), axis=-1, keepdims=True)
    return ((xf - mu) * lax.rsqrt(var + EPS) * gain.astype(jnp.float32)).astype(x.dtype)

def l2norm(x):
    xf = x.astype(jnp.float32)
    return xf * lax.rsqrt(jnp.sum(jnp.square(xf), axis=-1, keepdims=True) + EPS)

def ada_params(cond, w_ada, b_ada):
    return jnp.split(jax.nn.silu(cond) @ w_ada + b_ada, 6, axis=-1)

def centred_conv(x, w):
    pad = B_CONV // 2
    return lax.conv_general_dilated(
        x, w[:, None, :].astype(x.dtype), window_strides=(1,), padding=[(pad, pad)],
        dimension_numbers=('NWC', 'WIO', 'NWC'), feature_group_count=x.shape[-1])

def spatial_gating(u, v, n_chunks, ln_gain, w_s, b_s):
    u = jax.nn.gelu(u)
    v = layernorm(jax.nn.gelu(v), ln_gain)
    bn = v.shape[0]
    vc = v.reshape(bn, n_chunks, A_CHUNK, A_GROUPS, A_GROUP_DIM)
    mixed = jnp.einsum('gij,bnjgd->bnigd', w_s, vc) + b_s.T[None, None, :, :, None]
    return u * mixed.reshape(u.shape)

def gdn_prep(qkv, ab, conv_w, a_log, dt_bias):
    bn, t = qkv.shape[0], qkv.shape[1]
    qkv = jax.nn.silu(centred_conv(qkv, conv_w))
    q, k, v = jnp.split(qkv, 3, axis=-1)
    heads = lambda y: y.reshape(bn, t, B_HEADS, B_HEAD_DIM).transpose(0, 2, 1, 3)
    q = l2norm(heads(q)) * (B_HEAD_DIM ** -0.5)
    k = l2norm(heads(k))
    v = heads(v).astype(jnp.float32)
    a_f, b_f, a_b, b_b = ab.astype(jnp.float32).reshape(bn, t, 4, B_HEADS).transpose(2, 0, 3, 1)
    a_log = a_log.astype(jnp.float32)
    dt_bias = dt_bias.astype(jnp.float32)
    g_f = -jnp.exp(a_log[0])[:, None] * jax.nn.softplus(a_f + dt_bias[0][:, None])
    g_b = -jnp.exp(a_log[1])[:, None] * jax.nn.softplus(a_b + dt_bias[1][:, None])
    return q, k, v, (g_f, jax.nn.sigmoid(b_f)), (g_b, jax.nn.sigmoid(b_b))

def gated_delta_chunked(q, k, v, g, beta, s0):
    bn, h, t, dk = q.shape
    dv = v.shape[-1]
    c = B_CHUNK
    n = t // c
    f32 = jnp.float32
    q = q.astype(f32).reshape(bn, h, n, c, dk)
    k = k.astype(f32).reshape(bn, h, n, c, dk)
    v = v.astype(f32).reshape(bn, h, n, c, dv)
    beta = beta.astype(f32).reshape(bn, h, n, c, 1)
    gc = jnp.cumsum(g.astype(f32).reshape(bn, h, n, c), axis=-1)
    incl = jnp.tril(jnp.ones((c, c), dtype=bool))
    strict = jnp.tril(jnp.ones((c, c), dtype=bool), -1)
    decay = jnp.exp(jnp.where(incl, gc[..., :, None] - gc[..., None, :], -jnp.inf))
    k_beta = k * beta
    m = jnp.where(strict, jnp.einsum('bhnik,bhnjk->bhnij', k_beta, k) * decay, 0.0)
    eye = jnp.eye(c, dtype=f32)
    t_inv = lax.linalg.triangular_solve(eye + m, jnp.broadcast_to(eye, m.shape),
                                        left_side=True, lower=True, unit_diagonal=True)
    u_val = t_inv @ (v * beta)
    w_key = t_inv @ (k_beta * jnp.exp(gc)[..., None])
    intra = jnp.einsum('bhnik,bhnjk->bhnij', q, k) * decay
    q_dec = q * jnp.exp(gc)[..., None]
    k_dec = k * jnp.exp(gc[..., -1:] - gc)[..., None]
    g_tot = jnp.exp(gc[..., -1])[..., None, None]
    xs = tuple(jnp.moveaxis(y, 2, 0) for y in (intra, u_val, w_key, q_dec, k_dec, g_tot))

    def step(s, inp):
        a_n, u_n, w_n, qd_n, kd_n, gt_n = inp
        v_new = u_n - w_n @ s
        o_n = qd_n @ s + a_n @ v_new
        s = s * gt_n + jnp.einsum('bhck,bhcv->bhkv', kd_n, v_new)
        return s, o_n

    s_final, o = lax.scan(step, s0, xs)
    return jnp.moveaxis(o, 0, 2).reshape(bn, h, t, dv), s_final

def gated_delta_reverse(q, k, v, g, beta, s0):
    o, s = gated_delta_chunked(jnp.flip(q, 2), jnp.flip(k, 2), jnp.flip(v, 2),
                               jnp.flip(g, -1), jnp.flip(beta, -1), s0)
    return jnp.flip(o, 2), s

def gdn_output(o, z, gain):
    bn, h, t, dv = o.shape
    o = o.transpose(0, 2, 1, 3)
    o = o * lax.rsqrt(jnp.mean(jnp.square(o), axis=-1, keepdims=True) + EPS) * gain.astype(jnp.float32)
    o = o * jax.nn.silu(z.astype(jnp.float32).reshape(bn, t, h, dv))
    return o.reshape(bn, t, h * dv).astype(z.dtype)

def merge_branches(u, v, n_chunks, o_gdn, z, gate_a, gate_b, a_ln_g, a_w_s, a_b_s, b_norm_g, w_pa, w_pb, w_out):
    y_a = spatial_gating(u, v, n_chunks, a_ln_g, a_w_s, a_b_s) @ w_pa
    y_b = gdn_output(o_gdn, z, b_norm_g) @ w_pb
    return (jax.nn.sigmoid(gate_a) * y_a + jax.nn.sigmoid(gate_b) * y_b) @ w_out

def token_mixer(h_l, h_c, n_chunks_l, n_chunks_c, with_ctx, w_in, a_ln_g, a_w_s, a_b_s,
                conv_w, a_log, dt_bias, b_norm_g, w_pa, w_pb, w_out):
    u_l, v_l, qkv_l, z_l, ab_l, ga_l, gb_l = jnp.split(h_l @ w_in, IN_SPLITS, axis=-1)
    u_c, v_c, qkv_c, z_c, ab_c, ga_c, gb_c = jnp.split(h_c @ w_in, IN_SPLITS, axis=-1)
    qc, kc, vc, fwd_c, bwd_c = gdn_prep(qkv_c, ab_c, conv_w, a_log, dt_bias)
    ql, kl, vl, fwd_l, bwd_l = gdn_prep(qkv_l, ab_l, conv_w, a_log, dt_bias)
    bn = h_l.shape[0]
    s0 = jnp.zeros((bn, B_HEADS, B_HEAD_DIM, B_HEAD_DIM), jnp.float32)
    oc_f, s_f = gated_delta_chunked(qc, kc, vc, fwd_c[0], fwd_c[1], s0)
    oc_b, s_b = gated_delta_reverse(qc, kc, vc, bwd_c[0], bwd_c[1], s0)
    ol_f, _ = gated_delta_chunked(ql, kl, vl, fwd_l[0], fwd_l[1], s_f)
    ol_b, _ = gated_delta_reverse(ql, kl, vl, bwd_l[0], bwd_l[1], s_b)
    y_l = merge_branches(u_l, v_l, n_chunks_l, ol_f + ol_b, z_l, ga_l, gb_l,
                         a_ln_g, a_w_s, a_b_s, b_norm_g, w_pa, w_pb, w_out)
    y_c = None
    if with_ctx:
        y_c = merge_branches(u_c, v_c, n_chunks_c, oc_f + oc_b, z_c, ga_c, gb_c,
                             a_ln_g, a_w_s, a_b_s, b_norm_g, w_pa, w_pb, w_out)
    return y_l, y_c

def routed_moe(h, w_router, b_router, w1, w3, w2):
    scores = jax.nn.sigmoid(h.astype(jnp.float32) @ w_router.astype(jnp.float32))
    sel = scores + b_router.astype(jnp.float32)
    grp_score = jnp.sum(lax.top_k(sel.reshape(-1, N_GROUPS, EXPERTS_PER_GROUP), TOP_K)[0], axis=-1)
    best = jnp.argmax(grp_score, axis=-1)
    in_group = (jnp.arange(N_EXPERTS)[None, :] // EXPERTS_PER_GROUP) == best[:, None]
    _, idx = lax.top_k(jnp.where(in_group, sel, -jnp.inf), TOP_K)
    wts = jnp.take_along_axis(scores, idx, axis=-1)
    wts = wts / jnp.sum(wts, axis=-1, keepdims=True)
    combine = jnp.sum(jax.nn.one_hot(idx, N_EXPERTS, dtype=jnp.float32) * wts[..., None], axis=1).astype(h.dtype)
    y = jnp.zeros_like(h)
    for e in range(N_EXPERTS):
        y_e = (jax.nn.silu(h @ w1[e]) * (h @ w3[e])) @ w2[e]
        y = y + combine[:, e:e + 1] * y_e
    return y

def setup_inputs(seed: int = 0) -> dict:
    key = jax.random.key(seed)
    ks = jax.random.split(key, 26)
    nrm = lambda k, shape, scale: scale * jax.random.normal(k, shape, jnp.float32)
    L = DEPTH
    a_log = jnp.log(jax.random.uniform(ks[12], (L, 2, B_HEADS), jnp.float32, 1.0, 16.0))
    dt = jnp.exp(jax.random.uniform(ks[13], (L, 2, B_HEADS), jnp.float32, math.log(1e-3), math.log(1e-1)))
    dt_bias = dt + jnp.log(-jnp.expm1(-dt))
    return {
        'x': nrm(ks[0], (BATCH, SEQ, D_MODEL), 1.0),
        'c': nrm(ks[1], (BATCH, D_MODEL), 1.0),
        'ctx': nrm(ks[2], (BATCH, CTX_LEN, D_MODEL), 1.0),
        'c_ctx': nrm(ks[3], (D_MODEL,), 1.0),
        'w_ada': nrm(ks[4], (L, D_MODEL, 6 * D_MODEL), 0.5 * D_MODEL ** -0.5),
        'b_ada': nrm(ks[5], (L, 6 * D_MODEL), 0.02),
        'norm1_g': 1.0 + nrm(ks[6], (L, D_MODEL), 0.02),
        'norm2_g': 1.0 + nrm(ks[7], (L, D_MODEL), 0.02),
        'w_in': nrm(ks[8], (L, D_MODEL, IN_COLS), D_MODEL ** -0.5),
        'a_ln_g': 1.0 + nrm(ks[9], (L, A_WIDTH), 0.02),
        'a_w_s': nrm(ks[10], (L, A_GROUPS, A_CHUNK, A_CHUNK), A_CHUNK ** -0.5),
        'a_b_s': 1.0 + nrm(ks[11], (L, A_GROUPS, A_CHUNK), 0.02),
        'b_conv_w': nrm(ks[14], (L, B_CONV, 3 * B_WIDTH), B_CONV ** -0.5),
        'b_A_log': a_log,
        'b_dt_bias': dt_bias,
        'b_norm_g': 1.0 + nrm(ks[15], (L, B_HEAD_DIM), 0.02),
        'w_proj_a': nrm(ks[16], (L, A_WIDTH, D_MODEL), A_WIDTH ** -0.5),
        'w_proj_b': nrm(ks[17], (L, B_WIDTH, D_MODEL), B_WIDTH ** -0.5),
        'w_out': nrm(ks[18], (L, D_MODEL, D_MODEL), D_MODEL ** -0.5),
        'w_router': nrm(ks[19], (D_MODEL, N_EXPERTS), D_MODEL ** -0.5),
        'b_router': nrm(ks[20], (N_EXPERTS,), 0.01),
        'w_e1': nrm(ks[21], (L, N_EXPERTS, D_MODEL, D_EXPERT), D_MODEL ** -0.5),
        'w_e3': nrm(ks[22], (L, N_EXPERTS, D_MODEL, D_EXPERT), D_MODEL ** -0.5),
        'w_e2': nrm(ks[23], (L, N_EXPERTS, D_EXPERT, D_MODEL), D_EXPERT ** -0.5),
        'final_g': 1.0 + nrm(ks[24], (D_MODEL,), 0.02),
    }

def reference(x, c, ctx, c_ctx, w_ada, b_ada, norm1_g, norm2_g, w_in, a_ln_g, a_w_s, a_b_s,
              b_conv_w, b_A_log, b_dt_bias, b_norm_g, w_proj_a, w_proj_b, w_out,
              w_router, b_router, w_e1, w_e3, w_e2, final_g):
    bn, t, d = x.shape
    rows = t // GRID_W
    n_chunks_l = rows // ROWS_PER_CHUNK
    n_chunks_c = ctx.shape[1] // A_CHUNK
    x_l, x_c = x, ctx
    for l in range(DEPTH):
        with_ctx = l < DEPTH - 1
        sh1_l, sc1_l, g1_l, sh2_l, sc2_l, g2_l = [m[:, None, :] for m in ada_params(c, w_ada[l], b_ada[l])]
        sh1_c, sc1_c, g1_c, sh2_c, sc2_c, g2_c = ada_params(c_ctx, w_ada[l], b_ada[l])
        h_l = rmsnorm(x_l, norm1_g[l]) * (1.0 + sc1_l) + sh1_l
        h_c = rmsnorm(x_c, norm1_g[l]) * (1.0 + sc1_c) + sh1_c
        y_l, y_c = token_mixer(h_l, h_c, n_chunks_l, n_chunks_c, with_ctx, w_in[l], a_ln_g[l], a_w_s[l], a_b_s[l],
                               b_conv_w[l], b_A_log[l], b_dt_bias[l], b_norm_g[l], w_proj_a[l], w_proj_b[l], w_out[l])
        x_l = x_l + g1_l * y_l
        h2_l = rmsnorm(x_l, norm2_g[l]) * (1.0 + sc2_l) + sh2_l
        if with_ctx:
            x_c = x_c + g1_c * y_c
            h2_c = rmsnorm(x_c, norm2_g[l]) * (1.0 + sc2_c) + sh2_c
            n_ctx_tok = h2_c.shape[0] * h2_c.shape[1]
            flat = jnp.concatenate([h2_c.reshape(-1, d), h2_l.reshape(-1, d)], axis=0)
            y2 = routed_moe(flat, w_router, b_router, w_e1[l], w_e3[l], w_e2[l])
            x_c = x_c + g2_c * y2[:n_ctx_tok].reshape(h2_c.shape)
            x_l = x_l + g2_l * y2[n_ctx_tok:].reshape(h2_l.shape)
        else:
            y2 = routed_moe(h2_l.reshape(-1, d), w_router, b_router, w_e1[l], w_e3[l], w_e2[l])
            x_l = x_l + g2_l * y2.reshape(h2_l.shape)
    return rmsnorm(x_l, final_g)


_drawn_inputs = setup_inputs


def setup_inputs(seed=0):
    import zlib

    import numpy as np

    out = dict(_drawn_inputs(seed))
    spreads = {}
    factors = {'ctx': 4.538,
     'c_ctx': 5.066,
     'norm1_g': 3.257,
     'a_ln_g': 18.683,
     'a_b_s': 20.521,
     'b_norm_g': 20.851,
     'final_g': 7.847,
     'norm2_g': 7.643,
     'b_router': 4.64}
    for name, (base, spread) in spreads.items():
        noise = np.random.default_rng([zlib.crc32(name.encode()), seed]).standard_normal(out[name].shape)
        drawn = base * np.exp(spread * noise) if base else spread * noise
        out[name] = __import__('jax').numpy.asarray(drawn.astype(out[name].dtype))
    for name, factor in factors.items():
        out[name] = (out[name] * factor).astype(out[name].dtype)
    return out
```

```python
from contextlib import ExitStack

import concourse.bass as bass
from concourse import mybir

F32 = mybir.dt.float32
F32R = mybir.dt.float32r
BF16 = mybir.dt.bfloat16
ALU = mybir.AluOpType
ACT = mybir.ActivationFunctionType
AX = mybir.AxisListType.X

P = 128
D = 1024
KC = D // P
SEQ = 256
CTX = 256
TILES = (SEQ + CTX) // P
LAT = CTX // P
HEADS = 8
PAIRS = HEADS // 2
DIRS = 2
EPS = 1e-6
EXPERTS = 16
GROUPS = 4
PER_GROUP = EXPERTS // GROUPS
DE = 512
N = 512
RING = 4
SLOTS = P
UNIT = 2048
LEVELS = [2, 4, 8, 16, 32, 64]

COL_U, COL_V, COL_Q, COL_K, COL_VV, COL_Z = 0, D, 2 * D, 3 * D, 4 * D, 5 * D
COL_AB = 6 * D
COL_GA, COL_GB = COL_AB + 4 * HEADS, COL_AB + 4 * HEADS + D
CUM, BETA, NEG_BETA_EXP, EXP_CUM, EXP_REST, EXP_TOTAL, LOG_DECAY = range(7)


class Order:

    def __init__(self, engine, semaphore):
        self.engine, self.semaphore = engine, semaphore
        self.count, self.turn, self.per = 0, None, 0

    def mark(self, instruction):
        instruction.then_inc(self.semaphore, 1)
        self.count += 1

    def settle(self):
        value = self.count if self.turn is None else self.turn * self.per + self.count
        self.engine.wait_ge(self.semaphore, value)

    def after(self, instruction):
        self.mark(instruction)
        self.settle()

    def enter(self, turn, per):
        self.turn, self.per, self.before = turn, per, self.count

    def leave(self, turns):
        assert self.count - self.before == self.per, (self.count - self.before, self.per)
        self.count, self.turn = self.before + self.per * turns, None


def block_kernel(nc, x, c, ctx, c_ctx, w_ada, b_ada, norm1_g, norm2_g, w_in, a_ln_g, a_w_s, a_b_s,
                 b_conv_w, b_A_log, b_dt_bias, b_norm_g, w_proj_a, w_proj_b, w_out,
                 w_router, b_router, w_e1, w_e3, w_e2, final_g, out):
    stack = ExitStack()
    with stack:
        def sb(name, shape, dt=F32):
            return stack.enter_context(nc.sbuf_tensor(name, shape, dt))

        def sem(name):
            return stack.enter_context(nc.semaphore(name))

        ident = sb("ident", [P, P])
        ones = sb("ones", [P, P])
        causal = sb("causal", [P, DIRS, P])
        pair_mask = sb("pair_mask", [P, DIRS, P], BF16)
        level_mask = sb("level_mask", [P, len(LEVELS), DIRS, P], BF16)
        half_neg = sb("half_neg", [P, 2 * HEADS])
        rows = sb("rows", [40, P])
        cols = sb("cols", [P, 40])
        conv_col = sb("conv_col", [P, 3, HEADS, 5])
        conv_w = sb("conv_w", [P, 3, 2, 5])
        ada_tmp = sb("ada_tmp", [P, KC, 2])
        gain1 = sb("gain1", [P, KC, 2])
        shift1 = sb("shift1", [P, KC, 2])
        stat = sb("stat", [P, 3, TILES])
        raw = [sb(f"raw{r}", [P, UNIT]) for r in range(RING)]
        w_hi = [sb(f"w_hi{r}", [P, UNIT], F32R) for r in range(2)]
        w_lo = [sb(f"w_lo{r}", [P, UNIT], F32R) for r in range(2)]
        hT_hi = sb("hT_hi", [P, KC, TILES * P], F32R)
        hT_lo = sb("hT_lo", [P, KC, TILES * P], F32R)
        ab_hi = sb("ab_hi", [P, KC, 32], F32R)
        ab_lo = sb("ab_lo", [P, KC, 32], F32R)
        zo = sb("zo", [P, 4 * D])
        z_nat = zo[:, 0:2 * D].rearrange("p (t n) -> p t n", t=2)
        o_nat = zo[:, 2 * D:4 * D].rearrange("p (t h n) -> p t h n", t=2, h=HEADS)
        ada_vec = zo[:, :].rearrange("p (m n) -> p m n", m=4)
        gates = sb("gates", [P, 7, TILES, HEADS, DIRS])
        gate_row = sb("gate_row", [P, 2, DIRS, HEADS])
        pair_gates = sb("pair_gates", [P, 7, TILES, 2, DIRS])
        key_sq = sb("key_sq", [P, 4, TILES])
        guard = sb("guard", [P, TILES])
        key_lin = sb("key_lin", [P, 4, TILES])
        key_rs = sb("key_rs", [P, 4, TILES])
        cond_hi = sb("cond_hi", [P, KC, P], F32R)
        cond_lo = sb("cond_lo", [P, KC, P], F32R)
        mix_bias = sb("mix_bias", [P, HEADS])
        o_stat = sb("o_stat", [P, 3, 2 * HEADS])
        ln_stat = sb("ln_stat", [P, 2, 12])
        ln_mv = sb("ln_mv", [P, 2, 2])
        ln_rs = sb("ln_rs", [P, 2, 2])
        x_stat = sb("x_stat", [P, 3, 4])
        router_hi = sb("router_hi", [P, KC, EXPERTS], F32R)
        router_lo = sb("router_lo", [P, KC, EXPERTS], F32R)
        router_bias = sb("router_bias", [P, EXPERTS])
        score = sb("score", [P, 2, EXPERTS])
        choice = sb("choice", [P, 2, EXPERTS])
        chosen = sb("chosen", [P, 2, EXPERTS])
        place = sb("place", [P, 2, EXPERTS])
        cmp_a = sb("cmp_a", [P, 2 * GROUPS, PER_GROUP, PER_GROUP])
        cmp_b = sb("cmp_b", [P, 2 * GROUPS, PER_GROUP, PER_GROUP])
        rank = sb("rank", [P, 2 * GROUPS, PER_GROUP])
        group_score = sb("group_score", [P, 2, GROUPS])
        group_rank = sb("group_rank", [P, 2, GROUPS])
        token_sum = sb("token_sum", [P, 2, 2])
        order_mask = sb("before", [P, 3, PER_GROUP, PER_GROUP])
        slot_iota = sb("slot_iota", [P, 2 * P])
        overflow = sb("overflow", [P, 2])
        overflow_int = sb("overflow_int", [P, 1], mybir.dt.int32)
        zero_bf = sb("zero_bf", [P, N], BF16)
        arena_hi = sb("arena_hi", [P, 8 * 512])
        early = ExitStack()

        def sb_early(name, shape, dt=F32):
            return early.enter_context(nc.sbuf_tensor(name, shape, dt))

        kT = sb_early("kT", [P, 2, TILES * P])
        k_nat = sb_early("k_nat", [P, 2, TILES, P])
        v_nat = sb_early("v_nat", [P, 2, TILES, P])
        qT = sb_early("qT", [P, 2, 2 * P])
        arena = sb_early("arena", [P, 20 * 512])
        early.close()
        h2_hi = sb("h2_hi", [P, 2, D], F32R)
        h2_lo = sb("h2_lo", [P, 2, D], F32R)
        w_hi3 = sb("w_hi3", [P, UNIT], F32R)
        w_lo3 = sb("w_lo3", [P, UNIT], F32R)
        pick = [sb(f"pick{g}", [P, 2, 2, P], F32R) for g in range(2)]
        spread = [sb(f"spread{g}", [P, 2, 2 * P], F32R) for g in range(2)]
        slot_weight = sb("slot_weight", [P, 2, 2])
        act_hi = sb("act_hi", [P, 4, P], F32R)
        act_lo = sb("act_lo", [P, 4, P], F32R)
        y_hi = sb("y_hi", [P, D], F32R)
        y_lo = sb("y_lo", [P, D], F32R)
        e_hi = [w_hi[0], w_hi[1], w_hi3]
        e_lo = [w_lo[0], w_lo[1], w_lo3]

        def part(at, n=1):
            if at >= 20:
                return arena_hi[:, (at - 20) * 512:(at - 20 + n) * 512]
            return arena[:, at * 512:(at + n) * 512]

        def problems(at):
            return part(at).rearrange("p (h d n) -> p h d n", h=2, d=2)

        m_nat = [problems(g) for g in range(4)]
        u_inv = [problems(4 + g) for g in range(4)]
        t_inv = [problems(8 + g) for g in range(4)]
        p_blk = [problems(12 + g) for g in range(4)]
        intra = [problems(16 + g) for g in range(2)]
        v_beta = [problems(18 + g) for g in range(2)]
        k_dec = [problems(20 + g) for g in range(2)]
        r_val, v_new, state, q_state = problems(22), problems(23), problems(24), problems(25)
        o_step = [problems(26 + g) for g in range(2)]
        chan = [part(g) for g in range(6)]
        tanh_buf = [part(6 + g) for g in range(2)]
        sq_junk = part(8)
        x_nat = arena[:, 0:TILES * D].rearrange("p (t n) -> p t n", t=TILES)
        x_sq = arena[:, TILES * D:(TILES + 1) * D]
        h_full = [part(12 + g) for g in range(2)]
        ada_row = part(14, 4)[0:2, :]
        conv_rows = part(18)[0:120, 0:P]
        ab_raw = part(19)[:, 0:KC * 32].rearrange("p (c n) -> p c n", c=KC)
        gate_tmp = part(19)[:, KC * 32:2 * KC * 32].rearrange("p (k t h d) -> p k t h d", k=4, t=TILES, h=HEADS)

        def tokens(at):
            return part(at, 4).rearrange("p (t n) -> p t n", t=2)

        gate_a, u_act, v_act, gate_b, merged = tokens(0), tokens(4), tokens(8), tokens(12), tokens(16)
        o_sq, z_tanh = part(12, 4), part(16, 4)
        product = part(0, 4)
        x_lat, h2 = tokens(20), tokens(24)
        mix_raw = part(24, 2).rearrange("p (g n) -> p g n", g=HEADS)
        mix_T = part(26, 2).rearrange("p (g n) -> p g n", g=HEADS)
        ln_gain = kT[:, :, :].rearrange("p h n -> p (h n)")
        gain2 = k_nat[:, :, :, :].rearrange("p h t n -> p (h t n)")
        head_gain = qT[:, 0, 0:P]
        router_raw = v_nat[:, 0, 0, :].rearrange("p (c n) -> p c n", c=KC)
        silu_gate, act_nat = part(24), part(25)

        bank = [stack.enter_context(nc.psum_tensor(f"bank{b}", [P, N], F32)) for b in range(8)]

        s = {n: sem(n) for n in (
            "landed_x landed_small landed_conv landed_gate landed_ab consts_ready squares_ready power_ready x_normed "
            "rows_ready cols_ready cols_copied ada_used ada_row_copied ada_turned gains_ready "
            "xT_ready h_affine h_split conv_turned conv_ready act_own dve_own pool_own "
            "ab_split ab_sum gate_dve gate_act gate_sum "
            "hi_ready unit_split proj_ready tap_center taps_done tanh_done chan_ready "
            "chan_turned ksq_ready knorm_ready k_normed v_copied back_turned back_copied z_copied "
            "pair_ready scores_ready decay_lin decay_exp m_ready t_first u_turned u_copied "
            "p_sum p_masked up_sum u_updated t_turned t_copied "
            "step_ready ks_sum r_ready qs_sum qs_copied vnew_sum vnew_copied intra_sum o_part "
            "s_sum s_ready pair_free stored "
            "landed_cond landed_mix landed_xlat landed_ln landed_gain2 landed_head landed_ada landed_router landed_final "
            "cond_split unit_used drained_act drained_dve mix_turned mix_copied bias_turned "
            "o_squared o_power z_tanhed o_gated v_moments v_power v_normed mix_sum sgu_ready merge_ready "
            "turned turned_hi turned_lo x1_ready x1_squared x1_power h2_ready h2_rounded h2_split "
            "logits_sum logits_exp chosen_ready counts_sum picks_ready overflow_ready "
            "spread_sum spread_copied gathered gathered_hi gathered_lo silu_done act_done act_turned act_rounded act_split "
            "y_rounded y_split scattered x2_ready x2_squared x2_power out_ready sum_closed"
        ).split()}
        landed = [sem(f"landed{r}") for r in range(RING)]

        block = stack.enter_context(nc.Block())

        ada_v = w_ada[0].rearrange("(c p) n -> p c n", p=P)
        in_v = w_in[0].rearrange("(c p) n -> p c n", p=P)
        ADA_UNITS = 2 * D // 256
        LOOP_COL = [COL_K, COL_VV, COL_Q, COL_Z]
        CONV_KIND = [1, 2, 0]
        N_LEVELS = len(LEVELS)
        LOOP_UNITS = PAIRS * RING
        ada4_v = w_ada[0].rearrange("(h c p) n -> h p c n", h=2, p=P)
        in4_v = w_in[0].rearrange("(h c p) n -> h p c n", h=2, p=P)
        CHUNKS = [(in4_v, COL_GA), (in4_v, COL_GA + N), (in4_v, COL_U), (in4_v, COL_U + N),
                  (in4_v, COL_V), (in4_v, COL_V + N), (in4_v, COL_GB), (in4_v, COL_GB + N)]
        CHUNKS += [(w_proj_b[0].rearrange("(h c p) n -> h p c n", h=2, p=P), n * N) for n in range(2)]
        CHUNKS += [(w_proj_a[0].rearrange("(h c p) n -> h p c n", h=2, p=P), n * N) for n in range(2)]
        CHUNKS += [(ada4_v, 2 * D + n * N) for n in range(8)]
        CHUNKS += [(w_out[0].rearrange("(h c p) n -> h p c n", h=2, p=P), n * N) for n in range(2)]
        PB, PA, ADA, WO = 8, 10, 12, 20
        MERGE_UNITS = 2 * len(CHUNKS)
        SLOT_FILLS = ADA_UNITS // RING + PAIRS
        e1_v = w_e1[0].rearrange("e (c p) n -> p (e c) n", p=P)
        e3_v = w_e3[0].rearrange("e (c p) n -> p (e c) n", p=P)
        e2_v = w_e2[0].rearrange("e (c p) n -> p (e c) n", p=P)
        TURNS = EXPERTS // 4
        UP = [[(v, q, kh) for v in (e1_v, e3_v) for kh in range(2)] for q in range(4)]
        DOWN = [[(e2_v, q, nh) for nh in range(2)] for q in range(4)]
        TURN_UNITS = UP[0] + UP[1] + DOWN[0] + UP[2] + DOWN[1] + UP[3] + DOWN[2] + DOWN[3]
        UP_AT = [TURN_UNITS.index(UP[q][0]) for q in range(4)]
        DOWN_AT = [TURN_UNITS.index(DOWN[q][0]) for q in range(4)]
        PER_TURN = len(TURN_UNITS)

        def four(t):
            return t[:, :].rearrange("p (c n) -> p c n", c=4)

        def chunk_at(pos, d):
            return pos if d == 0 else pos ^ 1

        def wide(t):
            return t[:, :].rearrange("p (c n) -> p c n", c=KC)

        def by_pair(b):
            return b[:, :].rearrange("p (h d n) -> p h d n", h=2, d=2)

        @block.sync
        def _(sp):
            def load(dst, src, done):
                sp.dma_start(dst, src).then_inc(done, 16)

            load(rows[0:8, :], c[0].rearrange("(k p) -> k p", p=P), s["landed_small"])
            load(rows[8:16, :], c_ctx.rearrange("(k p) -> k p", p=P), s["landed_small"])
            load(rows[16:24, :], norm1_g[0].rearrange("(k p) -> k p", p=P), s["landed_small"])
            load(rows[24:40, :], b_ada[0, 0:2 * D].rearrange("(k p) -> k p", p=P), s["landed_small"])
            for n in range(ADA_UNITS):
                if n >= RING:
                    sp.wait_ge(s["ada_used"], n - RING + 1)
                load(wide(raw[n % RING]), ada_v[:, :, 256 * n:256 * n + 256], landed[n % RING])
                if n == 1:
                    load(x_nat[:, 0:LAT, :], ctx[0].rearrange("(t p) n -> p t n", p=P), s["landed_x"])
                    load(x_nat[:, LAT:TILES, :], x[0].rearrange("(t p) n -> p t n", p=P), s["landed_x"])
                    load(conv_rows[:, :], b_conv_w[0].rearrange("j (k p) -> (j k) p", p=P), s["landed_conv"])
                    for n2, v in enumerate((b_A_log, b_dt_bias)):
                        load(gate_row[:, n2, :, :].rearrange("p d h -> p (d h)"),
                             v[0].rearrange("d h -> (d h)").partition_broadcast(P), s["landed_gate"])
                    load(ab_raw[:, :, :], in_v[:, :, COL_AB:COL_AB + 32], s["landed_ab"])
            for j in range(RING):
                sp.wait_ge(s["ada_used"], ADA_UNITS - RING + 1 + j)
                load(wide(raw[j]), in_v[:, :, LOOP_COL[j]:LOOP_COL[j] + 256], landed[j])
            with sp.Fori(1, PAIRS) as i:
                for j in range(RING):
                    sp.wait_ge(s["unit_split"], i * RING + (j + 1 - RING))
                    load(wide(raw[j]), in_v[:, :, bass.ds(i * 256 + LOOP_COL[j], 256)], landed[j])

            def merge_unit(u):
                v, col = CHUNKS[u // 2]
                sp.wait_ge(s["unit_split"], LOOP_UNITS + u - RING + 1)
                load(four(raw[u % RING]), v[u % 2, :, :, col:col + N], landed[u % RING])

            for u in range(4):
                merge_unit(u)
            sp.wait_ge(s["pair_free"], PAIRS + 1)
            load(mix_raw, a_w_s[0].rearrange("g i j -> i g j"), s["landed_mix"])
            load(rows[0:8, :], a_b_s[0], s["landed_mix"])
            load(head_gain, b_norm_g[0].partition_broadcast(P), s["landed_head"])
            load(x_lat, x[0].rearrange("(t p) n -> p t n", p=P), s["landed_xlat"])
            load(ln_gain, a_ln_g[0].partition_broadcast(P), s["landed_ln"])
            load(gain2, norm2_g[0].partition_broadcast(P), s["landed_gain2"])
            load(router_raw[:, :, :], w_router.rearrange("(c p) n -> p c n", p=P), s["landed_router"])
            load(router_bias[:, :], b_router.partition_broadcast(P), s["landed_router"])
            for u in range(4, 2 * ADA):
                merge_unit(u)
            sp.wait_ge(s["turned"], 4)
            sp.wait_ge(s["o_gated"], 1)
            load(zo[:, :], b_ada[0, 2 * D:6 * D].partition_broadcast(P), s["landed_ada"])
            for u in range(2 * ADA, MERGE_UNITS):
                merge_unit(u)

            def expert_turn(i, base):
                for k, (v, q, half) in enumerate(TURN_UNITS):
                    sp.wait_ge(s["unit_split"], i * PER_TURN + (LOOP_UNITS + MERGE_UNITS + base * PER_TURN + k - RING + 1))
                    if v is e2_v:
                        src = v[:, bass.ds(i * 16 + q * 4, 4), half * N:half * N + N]
                    else:
                        src = v[:, bass.ds(i * 32 + (q * 8 + half * 4), 4), :]
                    load(four(raw[k % RING]), src, landed[k % RING])

            with sp.Fori(0, TURNS) as i:
                expert_turn(i, 0)
            sp.wait_ge(s["h2_ready"], 1)
            load(ada_vec[:, 0, :], final_g.partition_broadcast(P), s["landed_final"])
            sp.wait_ge(s["overflow_ready"], 1)
            with sp.If(sp.value_load(overflow_int[0:1, 0:1], min_val=0, max_val=1) > 0):
                with sp.Fori(0, TURNS) as i:
                    expert_turn(i, TURNS)
            sp.wait_ge(s["out_ready"], 2)
            sp.dma_start(out[0].rearrange("(t p) n -> p t n", p=P), x_lat).then_inc(s["stored"], 16)
            sp.wait_ge(s["stored"], 16)

        @block.gpsimd
        def _(pool):
            own = Order(pool, s["pool_own"])
            own.mark(pool.memset(ident[:, :], 0.0))
            own.mark(pool.memset(causal[:, :, :], 1.0))
            own.mark(pool.memset(pair_mask[:, :, :], 0.0))
            own.mark(pool.memset(level_mask[:, :, :, :], 0.0))
            pool.memset(half_neg[:, :], -0.5)
            pool.memset(ones[:, :], 1.0)
            pool.memset(zero_bf[:, :], 0.0).then_inc(s["pair_free"], 1)
            pool.memset(guard[:, :], 4 * EPS)
            own.settle()
            own.after(pool.affine_select(out=ident[:, :], in_=ident[:, :], compare_op=ALU.not_equal, fill=1.0,
                                         base=0, pattern=[[-1, P]], channel_multiplier=1))
            for d, sign in ((0, 1), (1, -1)):
                own.after(pool.affine_select(out=causal[:, d, :], in_=causal[:, d, :], compare_op=ALU.is_ge,
                                             fill=0.0, base=0, pattern=[[sign, P]], channel_multiplier=-sign))

            def other_half(view, size, first_rows):
                blocks = P // (2 * size)
                at = 0 if first_rows else size
                own.after(pool.memset(view, 1.0))
                own.after(pool.affine_select(out=view, in_=view, compare_op=ALU.is_ge, fill=0.0, base=-at,
                                             pattern=[[-2 * size, blocks], [0, size]], channel_multiplier=1))
                own.after(pool.affine_select(out=view, in_=view, compare_op=ALU.is_ge, fill=0.0, base=at + size - 1,
                                             pattern=[[2 * size, blocks], [0, size]], channel_multiplier=-1))

            for d in range(DIRS):
                other_half(pair_mask[:, d, :].rearrange("p (b h x) -> p b h x", h=2, x=1)[:, :, d, :], 1, d == 1)
                for l, size in enumerate(LEVELS):
                    v = level_mask[:, l, d, :].rearrange("p (b h x) -> p b h x", h=2, x=size)
                    other_half(v[:, :, 1 - d, :], size, d == 0)
            for n, (fill, op, base, step) in enumerate(((0.0, ALU.is_ge, -1, 1), (0.0, ALU.is_ge, -1, -1),
                                                        (0.0, ALU.is_equal, 0, 1))):
                own.after(pool.memset(order_mask[:, n, :, :], -1e30 if n == 2 else 1.0))
                own.mark(pool.affine_select(out=order_mask[:, n, :, :], in_=order_mask[:, n, :, :], compare_op=op, fill=fill,
                                            base=base, pattern=[[step, PER_GROUP], [-step, PER_GROUP]],
                                            channel_multiplier=0))
            pool.iota(slot_iota[:, :], pattern=[[1, 2 * P]], base=0, channel_multiplier=0,
                      allow_small_or_imprecise_dtypes=True)
            pool.memset(key_lin[:, :, :], 0.0).then_inc(s["consts_ready"], 1)
            pool.wait_ge(s["squares_ready"], 1)
            own.after(pool.tensor_scalar(stat[:, 1, :], stat[:, 0, :], 1.0 / D, EPS, ALU.mult, ALU.add))
            pool.tensor_tensor(stat[:, 2, :], stat[:, 1, :], half_neg[:, 0:TILES], ALU.pow)\
                .then_inc(s["power_ready"], 1)

            with pool.Fori(0, PAIRS) as i:
                own.enter(i, 4)
                pool.wait_ge(s["pair_free"], i + 1)
                pool.wait_ge(s["conv_ready"], 1)
                pool.tensor_copy(conv_w[:, :, :, :], conv_col[:, :, bass.ds(i * 2, 2), :])
                pool.wait_ge(s["gate_dve"], 6)
                pool.tensor_copy(pair_gates[:, :, :, :, :].rearrange("p k t h d -> p (k t) (h d)"),
                                 gates[:, :, :, :, :].rearrange("p k t h d -> p (k t) (h d)")[:, :, bass.ds(i * 4, 4)])\
                    .then_inc(s["pair_ready"], 1)
                for n in range(4):
                    pool.wait_ge(s["ksq_ready"], i * 4 + (n + 1))
                    tiles = TILES if n < 2 else 2
                    own.after(pool.tensor_tensor(key_lin[:, n, 0:tiles], key_sq[:, n, 0:tiles], guard[:, 0:tiles],
                                                 ALU.add))
                    pool.tensor_tensor(key_rs[:, n, 0:tiles], key_lin[:, n, 0:tiles], half_neg[:, 0:tiles], ALU.pow)\
                        .then_inc(s["knorm_ready"], 1)
                pool.wait_ge(s["k_normed"], i * 4 + 2)
                pool.wait_ge(s["v_copied"], i * 2 + 2)
                for pos in range(TILES):
                    if pos >= 2:
                        pool.wait_ge(s["s_ready"], i * 3 + (pos - 1))
                    for d in range(DIRS):
                        t = chunk_at(pos, d)
                        last = pool.tensor_tensor(v_beta[pos % 2][:, :, d, :], v_nat[:, :, t, :],
                                                  pair_gates[:, BETA, t, :, d:d + 1].to_broadcast([P, 2, P]), ALU.mult)
                        if pos < TILES - 1:
                            last = pool.tensor_tensor(k_dec[pos % 2][:, :, d, :], k_nat[:, :, t, :],
                                                      pair_gates[:, EXP_REST, t, :, d:d + 1].to_broadcast([P, 2, P]),
                                                      ALU.mult)
                    last.then_inc(s["step_ready"], 1)
            own.leave(PAIRS)
            pool.wait_ge(s["o_squared"], 1)
            own.after(pool.tensor_scalar(o_stat[:, 1, :], o_stat[:, 0, :], 4.0 / P, 4 * EPS, ALU.mult, ALU.add))
            pool.tensor_tensor(o_stat[:, 2, :], o_stat[:, 1, :], half_neg[:, :], ALU.pow).then_inc(s["o_power"], 1)
            pool.wait_ge(s["v_moments"], 1)
            own.after(pool.tensor_scalar(ln_rs[:, 0, :], ln_mv[:, :, 1], EPS, None, ALU.add))
            pool.tensor_tensor(ln_rs[:, 1, :], ln_rs[:, 0, :], half_neg[:, 0:2], ALU.pow).then_inc(s["v_power"], 1)
            for at, squared, power in ((0, "x1_squared", "x1_power"), (2, "x2_squared", "x2_power")):
                pool.wait_ge(s[squared], 1)
                own.after(pool.tensor_scalar(x_stat[:, 1, at:at + 2], x_stat[:, 0, at:at + 2], 1.0 / D, EPS,
                                             ALU.mult, ALU.add))
                pool.tensor_tensor(x_stat[:, 2, at:at + 2], x_stat[:, 1, at:at + 2], half_neg[:, 0:2], ALU.pow)\
                    .then_inc(s[power], 1)

        @block.scalar
        def _(act):
            own = Order(act, s["act_own"])
            act.wait_ge(s["landed_small"], 64)
            act.activation(rows[0:16, :], rows[0:16, :], ACT.Silu).then_inc(s["rows_ready"], 1)
            act.wait_ge(s["landed_x"], 32)
            for t in range(TILES):
                ins = act.activation(x_sq, x_nat[:, t, :], ACT.Square, accum_out=stat[:, 0, t:t + 1])
                if t < TILES - 1:
                    own.after(ins)
                else:
                    ins.then_inc(s["squares_ready"], 1)
            act.wait_ge(s["cols_ready"], 1)
            act.copy(cols[:, :], bank[7][:, 0:40]).then_inc(s["cols_copied"], 1)
            act.wait_ge(s["conv_turned"], 1)
            act.copy(conv_col[:, :, :, :], bank[7][:, 64:184].rearrange("p (j k h) -> p k h j", k=3, h=HEADS))\
                .then_inc(s["conv_ready"], 1)
            for b in range(ADA_UNITS // 2):
                act.wait_ge(s["ada_used"], 2 * b + 2)
                act.copy(ada_row[:, N * b:N * b + N], bank[b][0:2, :]).then_inc(s["ada_row_copied"], 1)
            act.wait_ge(s["gains_ready"], 1)
            for kc in range(KC):
                act.wait_ge(s["xT_ready"], kc + 1)
                if kc >= 2:
                    act.wait_ge(s["h_split"], kc - 1)
                for src, at in ((1, 0), (0, CTX)):
                    ins = act.activation(h_full[kc % 2][:, at:at + 256], bank[5 + kc % 2][:, at:at + 256],
                                         ACT.Identity, bias=shift1[:, kc, src:src + 1], scale=gain1[:, kc, src:src + 1])
                ins.then_inc(s["h_affine"], 1)
            act.wait_ge(s["landed_gate"], 32)
            act.activation(gate_row[:, 0, :, :], gate_row[:, 0, :, :], ACT.Exp)
            act.wait_ge(s["gate_dve"], 1)
            own.after(act.activation(gate_tmp[:, 1, :, :, :], gate_tmp[:, 0, :, :, :], ACT.Abs))
            own.after(act.activation(gate_tmp[:, 1, :, :, :], gate_tmp[:, 1, :, :, :], ACT.Exp, scale=-1.0))
            act.activation(gate_tmp[:, 2, :, :, :], gate_tmp[:, 1, :, :, :], ACT.Ln, bias=1.0)
            act.activation(gates[:, BETA, :, :, :], gates[:, BETA, :, :, :], ACT.Exp, scale=-1.0)\
                .then_inc(s["gate_act"], 1)
            act.wait_ge(s["gate_dve"], 4)
            act.activation(gates[:, EXP_CUM, :, :, :], gates[:, CUM, :, :, :], ACT.Exp)
            act.activation(gates[:, EXP_REST, :, :, :], gates[:, EXP_REST, :, :, :], ACT.Exp)
            act.activation(gates[:, EXP_TOTAL, :, :, :], gates[:, EXP_TOTAL, :, :, :], ACT.Exp)\
                .then_inc(s["gate_act"], 1)

            with act.Fori(0, PAIRS) as i:
                act.wait_ge(s["pair_free"], i + 1)

                def split_high(j):
                    act.wait_ge(landed[j], i * 16 + (16 + 16 * (ADA_UNITS // RING)))
                    if j >= 2:
                        act.wait_ge(s["proj_ready"], i * 8 + (2 * j - 2))
                    act.copy(w_hi[j % 2][:, :], raw[j][:, :]).then_inc(s["hi_ready"], 1)

                def center(n):
                    w = 512 if n < 4 else 256
                    act.wait_ge(s["proj_ready"], i * 8 + (n + 1))
                    act.activation(chan[n][:, 0:w], bank[n % 4][:, 0:w], ACT.Copy,
                                   scale=conv_w[:, CONV_KIND[n // 2], n % 2, 2:3]).then_inc(s["tap_center"], 1)

                def tanh(n):
                    w = 512 if n < 4 else 256
                    act.wait_ge(s["taps_done"], i * 6 + (n + 1))
                    if n >= 2:
                        act.wait_ge(s["chan_ready"], i * 6 + (n - 1))
                    act.activation(tanh_buf[n % 2][:, 0:w], chan[n][:, 0:w], ACT.Tanh, scale=0.5)\
                        .then_inc(s["tanh_done"], 1)

                def squares(n, key):
                    tiles = TILES if n < 4 else 2
                    act.wait_ge(s["chan_turned"], i * 6 + (n + 1))
                    for t in range(tiles):
                        ins = act.activation(sq_junk[:, t * P:(t + 1) * P], bank[4 + n % 2][:, t * P:(t + 1) * P],
                                             ACT.Square, accum_out=key_sq[:, key, t:t + 1])
                    ins.then_inc(s["ksq_ready"], 1)

                def back(n, key):
                    act.wait_ge(s["back_turned"], i * 4 + (key + 1))
                    if n < 4:
                        dst, src = kT[:, n, :], bank[6 + key % 2][:, :]
                    else:
                        dst, src = qT[:, n - 4, :], bank[6 + key % 2][:, 0:256]
                    act.mul(dst, src, 1.0 if n < 4 else P ** -0.5).then_inc(s["back_copied"], 1)

                act.wait_ge(s["pair_ready"], i + 1)
                split_high(0)
                split_high(1)
                center(0)
                center(1)
                split_high(2)
                tanh(0)
                tanh(1)
                squares(0, 0)

                center(2)
                center(3)
                split_high(3)
                act.wait_ge(s["ksq_ready"], i * 4 + 1)
                squares(1, 1)
                tanh(2)
                tanh(3)
                for n in (2, 3):
                    act.wait_ge(s["chan_turned"], i * 6 + (n + 1))
                    act.mul(v_nat[:, n - 2, :, :].rearrange("p t n -> p (t n)"), bank[4 + n % 2][:, :], 0.5)\
                        .then_inc(s["v_copied"], 1)
                center(4)
                center(5)
                back(0, 0)
                back(1, 1)
                tanh(4)
                tanh(5)
                act.wait_ge(s["ksq_ready"], i * 4 + 2)
                squares(4, 2)
                act.wait_ge(s["ksq_ready"], i * 4 + 3)
                squares(5, 3)
                for t in range(2):
                    act.wait_ge(s["proj_ready"], i * 8 + (7 + t))
                    act.copy(z_nat[:, t, bass.ds(i * 256, 256)], bank[2 + t][:, 0:256]).then_inc(s["z_copied"], 1)
                back(4, 2)
                back(5, 3)
                for g in range(TILES):
                    act.wait_ge(s["decay_lin"], i * 4 + (g + 1))
                    ins = act.activation(p_blk[g], p_blk[g], ACT.Exp, scale=-1.0)
                    if g >= LAT:
                        ins = act.activation(intra[g - LAT], intra[g - LAT], ACT.Exp)
                    ins.then_inc(s["decay_exp"], 1)
                for g in range(TILES):
                    act.wait_ge(s["u_turned"], i * 4 + (g + 1))
                    act.copy(u_inv[g], by_pair(bank[4 + g])).then_inc(s["u_copied"], 1)
                for l in range(N_LEVELS - 1):
                    for g in range(TILES):
                        act.wait_ge(s["t_turned"], i * 20 + (4 * l + g + 1))
                        act.copy(t_inv[g], by_pair(bank[4 + g])).then_inc(s["t_copied"], 1)
                for pos in range(TILES):
                    if pos >= LAT:
                        act.wait_ge(s["qs_sum"], i * 2 + (pos - LAT + 1))
                        if pos > LAT:
                            act.wait_ge(s["o_part"], i * 2 + (pos - LAT))
                        for h in range(2):
                            for d in range(DIRS):
                                t = chunk_at(pos, d)
                                ins = act.activation(q_state[:, h, d, :], by_pair(bank[6])[:, h, d, :], ACT.Copy,
                                                     scale=pair_gates[:, EXP_CUM, t, h, d:d + 1])
                        ins.then_inc(s["qs_copied"], 1)
                    act.wait_ge(s["vnew_sum"], i * 4 + (pos + 1))
                    act.copy(v_new, by_pair(bank[5])).then_inc(s["vnew_copied"], 1)

            def high(u):
                act.wait_ge(landed[u % RING], 16 * (SLOT_FILLS + u // RING + 1))
                if u >= 2:
                    act.wait_ge(s["unit_used"], u - 1)
                act.copy(w_hi[u % 2][:, :], raw[u % RING][:, :]).then_inc(s["hi_ready"], 1)

            def drain(chunk, dst, func, scale):
                act.wait_ge(s["unit_used"], 2 * chunk + 2)
                n = (chunk % 2) * N
                for t in range(2):
                    ins = act.activation(dst[:, t, n:n + N], bank[2 * (chunk % 2) + t][:, :], func, scale=scale)
                ins.then_inc(s["drained_act"], 1)

            def round_turned(at, first):
                for b in range(4):
                    act.wait_ge(s["turned"], first + b + 1)
                    act.copy(hT_hi[:, 2 * b:2 * b + 2, at:at + 256],
                             bank[4 + b][:, :].rearrange("p (c n) -> p c n", c=2)).then_inc(s["turned_hi"], 1)

            act.activation(cond_hi[:, :, :], cols[:, 0:8].unsqueeze(2).to_broadcast([P, KC, P]), ACT.Copy)\
                .then_inc(s["cond_split"], 1)
            high(0)
            high(1)
            act.wait_ge(s["pair_free"], PAIRS + 1)
            act.activation(z_tanh, zo[:, 0:2 * D], ACT.Tanh, scale=0.5).then_inc(s["z_tanhed"], 1)
            for b in range(2):
                act.wait_ge(s["mix_turned"], b + 1)
                act.copy(mix_T[:, 4 * b:4 * b + 4, :], bank[4 + b][:, :].rearrange("p (g n) -> p g n", g=4))\
                    .then_inc(s["mix_copied"], 1)
            act.wait_ge(s["bias_turned"], 1)
            act.copy(mix_bias[:, :], bank[6][:, 0:8]).then_inc(s["mix_copied"], 1)
            high(2)
            high(3)
            drain(0, gate_a, ACT.Tanh, 0.5)
            high(4)
            high(5)
            drain(1, gate_a, ACT.Tanh, 0.5)
            high(6)
            high(7)
            drain(2, u_act, ACT.Gelu_apprx_tanh, 1.0)
            round_turned(0, 0)
            high(8)
            high(9)
            drain(3, u_act, ACT.Gelu_apprx_tanh, 1.0)
            high(10)
            high(11)
            drain(4, v_act, ACT.Gelu_apprx_tanh, 1.0)
            high(12)
            high(13)
            drain(5, v_act, ACT.Gelu_apprx_tanh, 1.0)
            high(14)
            high(15)
            drain(6, gate_b, ACT.Tanh, 0.5)
            high(16)
            high(17)
            drain(7, gate_b, ACT.Tanh, 0.5)
            for u in range(18, 20):
                high(u)
            round_turned(256, 4)
            for u in range(20, 28):
                high(u)
            round_turned(0, 8)
            for u in range(28, MERGE_UNITS):
                high(u)
            act.wait_ge(s["x1_ready"], 1)
            for t in range(2):
                ins = act.activation(product[:, 0:D] if t == 0 else product[:, D:2 * D], x_lat[:, t, :], ACT.Square,
                                     accum_out=x_stat[:, 0, t:t + 1])
            ins.then_inc(s["x1_squared"], 1)
            act.wait_ge(s["h2_ready"], 1)
            act.copy(h2_hi[:, :, :], h2).then_inc(s["h2_rounded"], 1)
            round_turned(256, 12)
            act.wait_ge(s["logits_sum"], 1)
            act.activation(score[:, :, :], bank[0][:, 0:32].rearrange("p (t e) -> p t e", t=2), ACT.Exp, scale=-1.0)\
                .then_inc(s["logits_exp"], 1)

            def expert_turn(i, base):
                def at(n, per):
                    return i * per + (base * per + n)

                def high(k):
                    act.wait_ge(landed[k % RING], i * (16 * 6) + 16 * (SLOT_FILLS + MERGE_UNITS // RING + base * 6 + k // RING + 1))
                    act.wait_ge(s["unit_used"], i * PER_TURN + (MERGE_UNITS + base * PER_TURN + k - 2))
                    act.copy(e_hi[k % 3][:, :], raw[k % RING][:, :]).then_inc(s["hi_ready"], 1)

                def used(n):
                    act.wait_ge(s["unit_used"], i * PER_TURN + (MERGE_UNITS + base * PER_TURN + n))

                def gather(g):
                    act.wait_ge(s["spread_sum"], at(g + 1, 2))
                    act.copy(spread[g][:, :, :], bank[6][:, :].rearrange("p (e n) -> p e n", e=2))\
                        .then_inc(s["spread_copied"], 1)
                    for c in range(4):
                        act.wait_ge(s["gathered"], at(4 * g + c + 1, 8))
                        act.copy(hT_hi[:, 2 * c:2 * c + 2, 256 * g:256 * g + 256],
                                 bank[6 + (c + 1) % 2][:, :].rearrange("p (c n) -> p c n", c=2)).then_inc(s["gathered_hi"], 1)

                def silu(q):
                    used(UP_AT[q] + 2)
                    if q:
                        act.wait_ge(s["act_done"], at(q, 4))
                    act.activation(silu_gate, bank[4 + q % 2][:, :], ACT.Silu).then_inc(s["silu_done"], 1)

                def act_high(q):
                    act.wait_ge(s["act_turned"], at(q + 1, 4))
                    act.copy(act_hi[:, :, :], bank[4 + q % 2][:, :].rearrange("p (c n) -> p c n", c=4))\
                        .then_inc(s["act_rounded"], 1)

                def y_high(q, nh):
                    used(DOWN_AT[q] + nh + 1)
                    act.activation(y_hi[:, nh * N:nh * N + N], bank[7 - nh][:, :], ACT.Copy,
                                   scale=slot_weight[:, q // 2, q % 2:q % 2 + 1]).then_inc(s["y_rounded"], 1)

                high(0)
                high(1)
                gather(0)
                high(2)
                high(3)
                silu(0)
                high(4)
                high(5)
                gather(1)
                high(6)
                act_high(0)
                high(7)
                silu(1)
                high(8)
                high(9)
                high(10)
                y_high(0, 0)
                high(11)
                y_high(0, 1)
                high(12)
                act_high(1)
                high(13)
                silu(2)
                high(14)
                high(15)
                high(16)
                y_high(1, 0)
                high(17)
                y_high(1, 1)
                high(18)
                act_high(2)
                high(19)
                silu(3)
                high(20)
                high(21)
                high(22)
                y_high(2, 0)
                high(23)
                y_high(2, 1)
                act_high(3)
                y_high(3, 0)
                y_high(3, 1)

            act.wait_ge(s["unit_used"], MERGE_UNITS)
            with act.Fori(0, TURNS) as i:
                expert_turn(i, 0)
            act.wait_ge(s["overflow_ready"], 1)
            with act.If(act.value_load(overflow_int[0:1, 0:1], min_val=0, max_val=1) > 0):
                with act.Fori(0, TURNS) as i:
                    expert_turn(i, TURNS)
            act.wait_ge(s["x2_ready"], 1)
            for t in range(2):
                ins = act.activation(h2[:, t, :], x_lat[:, t, :], ACT.Square, accum_out=x_stat[:, 0, 2 + t:3 + t])
            ins.then_inc(s["x2_squared"], 1)

        @block.vector
        def _(dve):
            own = Order(dve, s["dve_own"])
            dve.wait_ge(s["ada_turned"], 1)
            ada_ps = bank[4][:, 0:32].rearrange("p (m s) -> p m s", s=2)
            dve.tensor_tensor(shift1[:, :, :], ada_ps[:, 0:8, :], cols[:, 24:32].unsqueeze(2).to_broadcast([P, KC, 2]), ALU.add)
            own.after(dve.tensor_tensor(ada_tmp[:, :, :], ada_ps[:, 8:16, :],
                                        cols[:, 32:40].unsqueeze(2).to_broadcast([P, KC, 2]), ALU.add))
            dve.scalar_tensor_tensor(out=gain1[:, :, :], in0=ada_tmp[:, :, :], scalar=1.0,
                                     in1=cols[:, 16:24].unsqueeze(2).to_broadcast([P, KC, 2]),
                                     op0=ALU.add, op1=ALU.mult).then_inc(s["gains_ready"], 1)
            dve.wait_ge(s["power_ready"], 1)
            for t in range(TILES):
                dve.tensor_scalar(x_nat[:, t, :], x_nat[:, t, :], stat[:, 2, t:t + 1], None, ALU.mult)\
                    .then_inc(s["x_normed"], 1)
            dve.wait_ge(s["landed_ab"], 16)
            own.after(dve.tensor_copy(ab_hi[:, :, :], ab_raw[:, :, :]))
            dve.tensor_tensor(ab_lo[:, :, :], ab_raw[:, :, :], ab_hi[:, :, :].bitcast(F32), ALU.subtract)\
                .then_inc(s["ab_split"], 1)
            for kc in range(KC):
                dve.wait_ge(s["h_affine"], kc + 1)
                own.after(dve.tensor_copy(hT_hi[:, kc, :], h_full[kc % 2]))
                dve.tensor_tensor(hT_lo[:, kc, :], h_full[kc % 2], hT_hi[:, kc, :].bitcast(F32), ALU.subtract)\
                    .then_inc(s["h_split"], 1)
            dve.wait_ge(s["ab_sum"], 1)
            dve.wait_ge(s["landed_gate"], 32)
            ab_ps = bank[4][:, 0:128].rearrange("p (t d x h) -> p t d x h", t=TILES, d=DIRS, x=2)

            def by_dir(t):
                return t.rearrange("p t h d -> p t d h")

            def over_tiles(t):
                return t.unsqueeze(1).to_broadcast([P, TILES, DIRS, HEADS])

            for t in range(TILES):
                dve.tensor_copy(by_dir(gates[:, BETA, :, :, :])[:, t], ab_ps[:, t, :, 1, :])
                ins = dve.tensor_tensor(by_dir(gate_tmp[:, 0, :, :, :])[:, t], ab_ps[:, t, :, 0, :],
                                        gate_row[:, 1, :, :], ALU.add)
            ins.then_inc(s["gate_dve"], 1)
            dve.wait_ge(s["gate_act"], 1)
            own.mark(dve.scalar_tensor_tensor(out=gate_tmp[:, 3, :, :, :], in0=gate_tmp[:, 0, :, :, :], scalar=0.0,
                                              in1=gate_tmp[:, 2, :, :, :], op0=ALU.max, op1=ALU.add))
            own.mark(dve.tensor_scalar(gate_row[:, 0, :, :], gate_row[:, 0, :, :], -1.0, None, ALU.mult))
            own.after(dve.tensor_scalar(gate_tmp[:, 1, :, :, :], gates[:, BETA, :, :, :], 1.0, None, ALU.add))
            for t in range(TILES):
                ins = dve.tensor_tensor(by_dir(gates[:, LOG_DECAY, :, :, :])[:, t], by_dir(gate_tmp[:, 3, :, :, :])[:, t],
                                        gate_row[:, 0, :, :], ALU.mult)
            ins.then_inc(s["gate_dve"], 1)
            dve.reciprocal(gates[:, BETA, :, :, :], gate_tmp[:, 1, :, :, :])
            dve.wait_ge(s["gate_sum"], 1)
            own.mark(dve.tensor_copy(gates[:, CUM, :, :, :].rearrange("p t h d -> p d (t h)"),
                                     bank[5][:, 0:64].rearrange("p (d n) -> p d n", d=DIRS)))
            own.after(dve.tensor_copy(gates[:, EXP_TOTAL, :, :, :].rearrange("p t h d -> p (t h d)"), bank[5][:, 64:128]))
            dve.tensor_tensor(gates[:, EXP_REST, :, :, :], gates[:, EXP_TOTAL, :, :, :], gates[:, CUM, :, :, :],
                              ALU.subtract).then_inc(s["gate_dve"], 2)
            dve.wait_ge(s["gate_act"], 2)
            dve.scalar_tensor_tensor(out=gates[:, NEG_BETA_EXP, :, :, :], in0=gates[:, BETA, :, :, :], scalar=-1.0,
                                     in1=gates[:, EXP_CUM, :, :, :], op0=ALU.mult, op1=ALU.mult)\
                .then_inc(s["gate_dve"], 2)

            with dve.Fori(0, PAIRS) as i:
                own.enter(i, 28)

                def split_low(j):
                    dve.wait_ge(s["hi_ready"], i * 4 + (j + 1))
                    dve.tensor_tensor(w_lo[j % 2][:, :], raw[j][:, :], w_hi[j % 2][:, :].bitcast(F32), ALU.subtract)\
                        .then_inc(s["unit_split"], 1)

                def taps(n):
                    w = 512 if n < 4 else 256
                    segs = w // 256
                    dve.wait_ge(s["tap_center"], i * 6 + (n + 1))
                    ps = bank[n % 4][:, 0:w].rearrange("p (s t) -> p s t", s=segs)
                    y = chan[n][:, 0:w].rearrange("p (s t) -> p s t", s=segs)
                    for tap in (0, 1, 3, 4):
                        o = tap - 2
                        a, b = max(0, -o), 256 - max(0, o)
                        ins = dve.scalar_tensor_tensor(out=y[:, :, a:b], in0=ps[:, :, a + o:b + o],
                                                       scalar=conv_w[:, CONV_KIND[n // 2], n % 2, tap:tap + 1],
                                                       in1=y[:, :, a:b], op0=ALU.mult, op1=ALU.add)
                        if tap < 4:
                            own.after(ins)
                    ins.then_inc(s["taps_done"], 1)

                def silu(n):
                    w = 512 if n < 4 else 256
                    dve.wait_ge(s["tanh_done"], i * 6 + (n + 1))
                    dve.scalar_tensor_tensor(out=chan[n][:, 0:w], in0=tanh_buf[n % 2][:, 0:w], scalar=1.0,
                                             in1=chan[n][:, 0:w], op0=ALU.add, op1=ALU.mult)\
                        .then_inc(s["chan_ready"], 1)

                def normed(n, key):
                    dve.wait_ge(s["knorm_ready"], i * 4 + (key + 1))
                    if n < 4:
                        dst, tiles = k_nat[:, n, :, :], TILES
                    else:
                        dst, tiles = chan[n - 4][:, 0:256].rearrange("p (t n) -> p t n", t=2), 2
                    dve.tensor_tensor(dst, bank[4 + n % 2][:, 0:tiles * P].rearrange("p (t n) -> p t n", t=tiles),
                                      key_rs[:, key, 0:tiles].unsqueeze(2).to_broadcast([P, tiles, P]), ALU.mult)\
                        .then_inc(s["k_normed"], 1)

                split_low(0)
                split_low(1)
                taps(0)
                taps(1)
                silu(0)
                silu(1)
                split_low(2)
                normed(0, 0)
                taps(2)
                taps(3)
                split_low(3)
                normed(1, 1)
                silu(2)
                silu(3)
                taps(4)
                taps(5)
                silu(4)
                silu(5)
                normed(4, 2)
                normed(5, 3)

                def decay_args(g):
                    dve.wait_ge(s["scores_ready"], i * 4 + (g + 1))
                    cum = by_pair(bank[6 + g % 2])
                    for h in range(2):
                        for d in range(DIRS):
                            own_cum = pair_gates[:, CUM, g, h, d:d + 1]
                            ins = dve.tensor_scalar(p_blk[g][:, h, d, :], cum[:, h, d, :], own_cum, 0.0,
                                                    ALU.subtract, ALU.max)
                            if g >= LAT:
                                ins = dve.tensor_scalar(intra[g - LAT][:, h, d, :], cum[:, h, d, :], own_cum, 0.0,
                                                        ALU.subtract, ALU.min)
                    ins.then_inc(s["decay_lin"], 1)

                def first_level(g):
                    dve.wait_ge(s["decay_exp"], i * 4 + (g + 1))
                    kk = bank[4 + g % 2][:, 0:256].rearrange("p (h n) -> p h n", h=2)
                    kq = bank[4 + g % 2][:, 256:512].rearrange("p (h n) -> p h n", h=2)
                    for h in range(2):
                        for d in range(DIRS):
                            ins = dve.scalar_tensor_tensor(out=m_nat[g][:, h, d, :], in0=kk[:, h, :],
                                                           scalar=pair_gates[:, BETA, g, h, d:d + 1],
                                                           in1=p_blk[g][:, h, d, :], op0=ALU.mult, op1=ALU.mult)
                    own.mark(ins)
                    if g >= LAT:
                        own.after(dve.tensor_tensor(intra[g - LAT], intra[g - LAT],
                                                    kq.unsqueeze(2).to_broadcast([P, 2, DIRS, P]), ALU.mult))
                        dve.tensor_tensor(intra[g - LAT], intra[g - LAT],
                                          causal[:, :, :].unsqueeze(1).to_broadcast([P, 2, DIRS, P]), ALU.mult)
                    else:
                        own.settle()
                    own.after(dve.tensor_tensor(p_blk[g], m_nat[g],
                                                pair_mask[:, :, :].unsqueeze(1).to_broadcast([P, 2, DIRS, P]), ALU.mult))
                    dve.tensor_tensor(t_inv[g].rearrange("p h d n -> p (h d) n"),
                                      ident[:, :].unsqueeze(1).to_broadcast([P, 4, P]),
                                      p_blk[g].rearrange("p h d n -> p (h d) n"), ALU.subtract)\
                        .then_inc(s["t_first"], 1)

                decay_args(0)
                decay_args(1)
                first_level(0)
                decay_args(2)
                first_level(1)
                decay_args(3)
                first_level(2)
                first_level(3)
                for l in range(N_LEVELS):
                    for g in range(TILES):
                        dve.wait_ge(s["p_sum"], i * 24 + (4 * l + g + 1))
                        dve.tensor_tensor(p_blk[g], by_pair(bank[4 + g]),
                                          level_mask[:, l, :, :].unsqueeze(1).to_broadcast([P, 2, DIRS, P]), ALU.mult)\
                            .then_inc(s["p_masked"], 1)
                    for g in range(TILES):
                        dve.wait_ge(s["up_sum"], i * 24 + (4 * l + g + 1))
                        dve.tensor_tensor(u_inv[g], u_inv[g], by_pair(bank[4 + g]), ALU.subtract)\
                            .then_inc(s["u_updated"], 1)
                for pos in range(TILES):
                    if pos:
                        dve.wait_ge(s["ks_sum"], i * 3 + pos)
                        dve.wait_ge(s["step_ready"], i * 4 + (pos + 1))
                        for h in range(2):
                            for d in range(DIRS):
                                t = chunk_at(pos, d)
                                ins = dve.scalar_tensor_tensor(out=r_val[:, h, d, :], in0=by_pair(bank[4])[:, h, d, :],
                                                               scalar=pair_gates[:, NEG_BETA_EXP, t, h, d:d + 1],
                                                               in1=v_beta[pos % 2][:, h, d, :],
                                                               op0=ALU.mult, op1=ALU.add)
                        ins.then_inc(s["r_ready"], 1)
                    if pos < TILES - 1:
                        dve.wait_ge(s["s_sum"], i * 3 + (pos + 1))
                        if pos == 0:
                            ins = dve.tensor_copy(state, by_pair(bank[4]))
                        else:
                            for h in range(2):
                                for d in range(DIRS):
                                    t = chunk_at(pos, d)
                                    ins = dve.scalar_tensor_tensor(out=state[:, h, d, :], in0=state[:, h, d, :],
                                                                   scalar=pair_gates[:, EXP_TOTAL, t, h, d:d + 1],
                                                                   in1=by_pair(bank[4])[:, h, d, :],
                                                                   op0=ALU.mult, op1=ALU.add)
                        ins.then_inc(s["s_ready"], 1)
                    if pos >= LAT:
                        dve.wait_ge(s["intra_sum"], i * 2 + (pos - LAT + 1))
                        dve.wait_ge(s["qs_copied"], i * 2 + (pos - LAT + 1))
                        own_ins = dve.tensor_tensor(o_step[pos - LAT], q_state, by_pair(bank[7]), ALU.add)
                        own_ins.then_inc(s["o_part"], 1)
                dve.wait_ge(s["o_part"], i * 2 + 2)
                for d in range(DIRS):
                    ins = dve.tensor_tensor(o_nat[:, chunk_at(TILES - 1, d) - LAT, bass.ds(i * 2, 2), :],
                                            o_step[1][:, :, d, :], o_step[0][:, :, 1 - d, :], ALU.add)
                ins.then_inc(s["pair_free"], 1)
            own.leave(PAIRS)

            def low(u):
                dve.wait_ge(s["hi_ready"], LOOP_UNITS + u + 1)
                dve.tensor_tensor(w_lo[u % 2][:, :], raw[u % RING][:, :], w_hi[u % 2][:, :].bitcast(F32), ALU.subtract)\
                    .then_inc(s["unit_split"], 1)

            def split_turned(at, first):
                for b in range(4):
                    dve.wait_ge(s["turned_hi"], first + b + 1)
                    dve.tensor_tensor(hT_lo[:, 2 * b:2 * b + 2, at:at + 256],
                                      bank[4 + b][:, :].rearrange("p (c n) -> p c n", c=2),
                                      hT_hi[:, 2 * b:2 * b + 2, at:at + 256].bitcast(F32), ALU.subtract)\
                        .then_inc(s["turned_lo"], 1)

            def used(chunk):
                dve.wait_ge(s["unit_used"], 2 * chunk + 2)

            o_heads = zo[:, 2 * D:4 * D].rearrange("p (m n) -> p m n", n=P)
            dve.wait_ge(s["cond_split"], 1)
            dve.tensor_tensor(cond_lo[:, :, :], cols[:, 0:8].unsqueeze(2).to_broadcast([P, KC, P]),
                              cond_hi[:, :, :].bitcast(F32), ALU.subtract).then_inc(s["cond_split"], 1)
            low(0)
            dve.wait_ge(s["pair_free"], PAIRS + 1)
            own.after(dve.tensor_tensor(o_sq, zo[:, 2 * D:4 * D], zo[:, 2 * D:4 * D], ALU.mult))
            low(1)
            dve.tensor_reduce(o_stat[:, 0, :], o_sq.rearrange("p (m n) -> p m n", n=P), AX, ALU.add)\
                .then_inc(s["o_squared"], 1)
            dve.wait_ge(s["z_tanhed"], 1)
            own.mark(dve.scalar_tensor_tensor(out=zo[:, 0:2 * D], in0=z_tanh, scalar=1.0, in1=zo[:, 0:2 * D],
                                              op0=ALU.add, op1=ALU.mult))
            low(2)
            dve.wait_ge(s["o_power"], 1)
            own.after(dve.tensor_tensor(o_heads, o_heads, o_stat[:, 2, :].unsqueeze(2).to_broadcast([P, 2 * HEADS, P]),
                                        ALU.mult))
            low(3)
            dve.wait_ge(s["landed_head"], 16)
            own.after(dve.tensor_tensor(o_heads, o_heads, head_gain.unsqueeze(1).to_broadcast([P, 2 * HEADS, P]),
                                        ALU.mult))
            low(4)
            dve.tensor_tensor(zo[:, 2 * D:4 * D], zo[:, 2 * D:4 * D], zo[:, 0:2 * D], ALU.mult).then_inc(s["o_gated"], 1)
            low(5)
            dve.wait_ge(s["landed_router"], 32)
            own.after(dve.tensor_copy(router_hi[:, :, :], router_raw[:, :, :]))
            dve.tensor_tensor(router_lo[:, :, :], router_raw[:, :, :], router_hi[:, :, :].bitcast(F32), ALU.subtract)
            low(6)
            low(7)
            split_turned(0, 0)
            for u in range(8, 14):
                low(u)
            dve.wait_ge(s["drained_act"], 6)
            for t in range(2):
                for n in range(2):
                    ins = dve.bn_stats(ln_stat[:, t, 6 * n:6 * n + 6], v_act[:, t, n * N:n * N + N])
            own.after(ins)
            for t in range(2):
                ins = dve.bn_aggr(ln_mv[:, t, :], ln_stat[:, t, :])
            ins.then_inc(s["v_moments"], 1)
            low(14)
            dve.wait_ge(s["v_power"], 1)
            for t in range(2):
                ins = dve.tensor_scalar(v_act[:, t, :], v_act[:, t, :], ln_mv[:, t, 0:1], ln_rs[:, 1, t:t + 1],
                                        ALU.subtract, ALU.mult)
            own.after(ins)
            low(15)
            dve.wait_ge(s["landed_ln"], 16)
            dve.tensor_tensor(v_act, v_act, ln_gain.unsqueeze(1).to_broadcast([P, 2, D]), ALU.mult)\
                .then_inc(s["v_normed"], 1)
            for u in range(16, 18):
                low(u)
            dve.wait_ge(s["mix_copied"], 3)
            for t in range(2):
                dve.wait_ge(s["mix_sum"], t + 1)
                for g in range(HEADS):
                    ins = dve.scalar_tensor_tensor(out=u_act[:, t, g * P:(g + 1) * P],
                                                   in0=bank[4 + 2 * t + g // 4][:, (g % 4) * P:(g % 4 + 1) * P],
                                                   scalar=mix_bias[:, g:g + 1], in1=u_act[:, t, g * P:(g + 1) * P],
                                                   op0=ALU.add, op1=ALU.mult)
            ins.then_inc(s["sgu_ready"], 1)
            low(18)
            low(19)

            def gated(chunk, gate, dst):
                used(chunk)
                n = (chunk % 2) * N
                for t in range(2):
                    ins = dve.scalar_tensor_tensor(out=dst[:, t, n:n + N], in0=gate[:, t, n:n + N], scalar=1.0,
                                                   in1=bank[2 * (chunk % 2) + t][:, :], op0=ALU.add, op1=ALU.mult)
                ins.then_inc(s["drained_dve"], 1)

            gated(PB, gate_b, merged)
            split_turned(256, 4)
            low(20)
            low(21)
            gated(PB + 1, gate_b, merged)
            low(22)
            low(23)
            gated(PA, gate_a, gate_a)
            low(24)
            low(25)
            gated(PA + 1, gate_a, gate_a)
            dve.wait_ge(s["drained_dve"], 4)
            dve.tensor_tensor(merged, merged, gate_a, ALU.add).then_inc(s["merge_ready"], 1)

            def ada(chunk):
                used(chunk)
                m = chunk - ADA
                dve.tensor_tensor(zo[:, m * N:m * N + N], bank[2 * (chunk % 2)][:, :], zo[:, m * N:m * N + N], ALU.add)\
                    .then_inc(s["drained_dve"], 1)

            dve.wait_ge(s["landed_ada"], 16)
            low(26)
            low(27)
            ada(12)
            split_turned(0, 8)
            for chunk in range(13, 20):
                low(2 * chunk + 2)
                low(2 * chunk + 3)
                ada(chunk)
            dve.wait_ge(s["landed_gain2"], 16)
            dve.wait_ge(s["drained_dve"], 12)
            dve.scalar_tensor_tensor(out=ada_vec[:, 2, :], in0=ada_vec[:, 2, :], scalar=1.0, in1=gain2,
                                     op0=ALU.add, op1=ALU.mult)
            low(42)
            low(43)
            dve.wait_ge(s["landed_xlat"], 16)
            for chunk in (WO, WO + 1):
                used(chunk)
                n = (chunk % 2) * N
                for t in range(2):
                    ins = dve.tensor_tensor(product[:, t * D + n:t * D + n + N], bank[2 * (chunk % 2) + t][:, :],
                                            ada_vec[:, 0, n:n + N], ALU.mult)
                own.after(ins)
                for t in range(2):
                    ins = dve.scalar_tensor_tensor(out=x_lat[:, t, n:n + N], in0=product[:, t * D + n:t * D + n + N],
                                                   scalar=0.5, in1=x_lat[:, t, n:n + N], op0=ALU.mult, op1=ALU.add)
            ins.then_inc(s["x1_ready"], 1)
            dve.wait_ge(s["x1_power"], 1)
            for t in range(2):
                ins = dve.scalar_tensor_tensor(out=h2[:, t, :], in0=x_lat[:, t, :], scalar=x_stat[:, 2, t:t + 1],
                                               in1=ada_vec[:, 2, :], op0=ALU.mult, op1=ALU.mult)
            own.after(ins)
            dve.tensor_tensor(h2, h2, ada_vec[:, 1, :].unsqueeze(1).to_broadcast([P, 2, D]), ALU.add)\
                .then_inc(s["h2_ready"], 1)
            split_turned(256, 12)
            dve.wait_ge(s["h2_rounded"], 1)
            dve.tensor_tensor(h2_lo[:, :, :], h2, h2_hi[:, :, :].bitcast(F32), ALU.subtract).then_inc(s["h2_split"], 1)
            dve.wait_ge(s["logits_exp"], 1)
            own.after(dve.tensor_scalar(choice[:, :, :], score[:, :, :], 1.0, None, ALU.add))
            own.after(dve.reciprocal(score[:, :, :], choice[:, :, :]))
            own.after(dve.tensor_tensor(choice[:, :, :], score[:, :, :],
                                        router_bias[:, :].unsqueeze(1).to_broadcast([P, 2, EXPERTS]), ALU.add))

            def beaten(values, count, dst):
                ours = values.unsqueeze(3).to_broadcast([P, count, 4, 4])
                theirs = values.unsqueeze(2).to_broadcast([P, count, 4, 4])
                own.mark(dve.tensor_tensor(cmp_a[:, 0:count], theirs, ours, ALU.is_ge))
                own.after(dve.tensor_tensor(cmp_b[:, 0:count], theirs, ours, ALU.is_gt))
                for buf, n in ((cmp_a, 0), (cmp_b, 1)):
                    ins = dve.tensor_tensor(buf[:, 0:count], buf[:, 0:count],
                                            order_mask[:, n, :, :].unsqueeze(1).to_broadcast([P, count, 4, 4]), ALU.mult)
                own.after(ins)
                own.after(dve.tensor_tensor(cmp_a[:, 0:count], cmp_a[:, 0:count], cmp_b[:, 0:count], ALU.add))
                own.after(dve.tensor_reduce(dst, cmp_a[:, 0:count], AX, ALU.add))

            by_group = choice[:, :, :].rearrange("p t (g e) -> p (t g) e", g=GROUPS)
            own.after(dve.tensor_tensor(cmp_a[:, :, :, :], by_group.unsqueeze(3).to_broadcast([P, 8, 4, 4]),
                                        by_group.unsqueeze(2).to_broadcast([P, 8, 4, 4]), ALU.add))
            own.after(dve.tensor_tensor(cmp_a[:, :, :, :], cmp_a[:, :, :, :],
                                        order_mask[:, 2, :, :].unsqueeze(1).to_broadcast([P, 8, 4, 4]), ALU.add))
            own.after(dve.tensor_reduce(group_score[:, :, :].rearrange("p t g -> p (t g)"),
                                        cmp_a[:, :, :, :].rearrange("p m i j -> p m (i j)"), AX, ALU.max))
            beaten(by_group, 8, rank[:, :, :])
            beaten(group_score[:, :, :], 2, group_rank[:, :, :])
            own.mark(dve.tensor_scalar(group_rank[:, :, :], group_rank[:, :, :], 0.5, None, ALU.is_lt))
            own.after(dve.tensor_scalar(rank[:, :, :], rank[:, :, :], 1.5, None, ALU.is_lt))
            dve.tensor_tensor(chosen[:, :, :].rearrange("p t (g e) -> p (t g) e", g=GROUPS), rank[:, :, :],
                              group_rank[:, :, :].rearrange("p t g -> p (t g)").unsqueeze(2).to_broadcast([P, 8, 4]),
                              ALU.mult).then_inc(s["chosen_ready"], 1)
            dve.wait_ge(s["chosen_ready"], 1)
            own.after(dve.tensor_tensor(score[:, :, :], score[:, :, :], chosen[:, :, :], ALU.mult))
            own.after(dve.tensor_reduce(token_sum[:, 0, :], score[:, :, :], AX, ALU.add))
            own.after(dve.reciprocal(token_sum[:, 1, :], token_sum[:, 0, :]))
            own.mark(dve.tensor_tensor(choice[:, :, :], score[:, :, :],
                                       token_sum[:, 1, :].unsqueeze(2).to_broadcast([P, 2, EXPERTS]), ALU.mult))
            dve.wait_ge(s["counts_sum"], 1)
            own.mark(dve.tensor_reduce(overflow[:, 0:1], bank[0][:, 64:80], AX, ALU.max))
            own.after(dve.tensor_tensor(place[:, :, :], bank[0][:, 32:64].rearrange("p (t e) -> p t e", t=2),
                                        chosen[:, :, :], ALU.subtract))
            dve.tensor_scalar(overflow_int[:, :], overflow[:, 0:1], SLOTS + 0.5, None, ALU.is_gt)\
                .then_inc(s["overflow_ready"], 1)

            def expert_turn(i, base):
                def at(n, per):
                    return i * per + (base * per + n)

                def low(k):
                    dve.wait_ge(s["hi_ready"], i * PER_TURN + (LOOP_UNITS + MERGE_UNITS + base * PER_TURN + k + 1))
                    dve.tensor_tensor(e_lo[k % 3][:, :], raw[k % RING][:, :], e_hi[k % 3][:, :].bitcast(F32), ALU.subtract)\
                        .then_inc(s["unit_split"], 1)

                def used(n):
                    dve.wait_ge(s["unit_used"], i * PER_TURN + (MERGE_UNITS + base * PER_TURN + n))

                def picks(g):
                    for t in range(2):
                        for e in range(2):
                            n = 2 * g + e
                            ins = dve.tensor_scalar(pick[g][:, t, e, :], slot_iota[:, base * P // TURNS:base * P // TURNS + P],
                                                    place[:, t, bass.ds(i * 4 + n, 1)], chosen[:, t, bass.ds(i * 4 + n, 1)],
                                                    ALU.is_equal, ALU.mult)
                    ins.then_inc(s["picks_ready"], 1)

                def gather(g):
                    dve.wait_ge(s["spread_copied"], at(g + 1, 2))
                    ins = dve.tensor_copy(slot_weight[:, g, :], bank[7][:, 0:2])
                    ins.then_inc(s["gathered_lo"], 1)
                    for c in range(4):
                        dve.wait_ge(s["gathered_hi"], at(4 * g + c + 1, 8))
                        dve.tensor_tensor(hT_lo[:, 2 * c:2 * c + 2, 256 * g:256 * g + 256],
                                          bank[6 + (c + 1) % 2][:, :].rearrange("p (c n) -> p c n", c=2),
                                          hT_hi[:, 2 * c:2 * c + 2, 256 * g:256 * g + 256].bitcast(F32), ALU.subtract)\
                            .then_inc(s["gathered_lo"], 1)

                def act_product(q):
                    used(UP_AT[q] + 4)
                    dve.wait_ge(s["silu_done"], at(q + 1, 4))
                    dve.tensor_tensor(act_nat, bank[5 - q % 2][:, :], silu_gate, ALU.mult).then_inc(s["act_done"], 1)

                def act_low(q):
                    dve.wait_ge(s["act_rounded"], at(q + 1, 4))
                    dve.tensor_tensor(act_lo[:, :, :], bank[4 + q % 2][:, :].rearrange("p (c n) -> p c n", c=4),
                                      act_hi[:, :, :].bitcast(F32), ALU.subtract).then_inc(s["act_split"], 1)

                def y_low(q, nh):
                    dve.wait_ge(s["y_rounded"], at(2 * q + nh + 1, 8))
                    dve.scalar_tensor_tensor(out=y_lo[:, nh * N:nh * N + N], in0=bank[7 - nh][:, :],
                                             scalar=slot_weight[:, q // 2, q % 2:q % 2 + 1],
                                             in1=y_hi[:, nh * N:nh * N + N].bitcast(F32),
                                             op0=ALU.mult, op1=ALU.subtract).then_inc(s["y_split"], 1)

                picks(0)
                low(0)
                low(1)
                gather(0)
                low(2)
                picks(1)
                low(3)
                low(4)
                act_product(0)
                low(5)
                gather(1)
                low(6)
                act_low(0)
                low(7)
                low(8)
                act_product(1)
                low(9)
                y_low(0, 0)
                low(10)
                y_low(0, 1)
                low(11)
                act_low(1)
                low(12)
                low(13)
                act_product(2)
                low(14)
                low(15)
                y_low(1, 0)
                low(16)
                y_low(1, 1)
                low(17)
                act_low(2)
                low(18)
                low(19)
                act_product(3)
                low(20)
                low(21)
                y_low(2, 0)
                low(22)
                y_low(2, 1)
                low(23)
                act_low(3)
                y_low(3, 0)
                y_low(3, 1)

            with dve.Fori(0, TURNS) as i:
                expert_turn(i, 0)
            dve.wait_ge(s["scattered"], 4 * TURNS)
            with dve.If(dve.value_load(overflow_int[0:1, 0:1], min_val=0, max_val=1) > 0):
                with dve.Fori(0, TURNS) as i:
                    expert_turn(i, TURNS)
                dve.wait_ge(s["scattered"], 8 * TURNS)
            dve.wait_ge(s["sum_closed"], 1)
            for t in range(2):
                for nh in range(2):
                    ins = dve.tensor_tensor(h2[:, t, nh * N:nh * N + N], bank[2 * t + nh][:, :],
                                            ada_vec[:, 3, nh * N:nh * N + N], ALU.mult)
            own.after(ins)
            dve.tensor_tensor(x_lat, x_lat, h2, ALU.add).then_inc(s["x2_ready"], 1)
            dve.wait_ge(s["landed_final"], 16)
            dve.wait_ge(s["x2_power"], 1)
            for t in range(2):
                dve.scalar_tensor_tensor(out=x_lat[:, t, :], in0=x_lat[:, t, :], scalar=x_stat[:, 2, 2 + t:3 + t],
                                         in1=ada_vec[:, 0, :], op0=ALU.mult, op1=ALU.mult).then_inc(s["out_ready"], 1)

        @block.tensor
        def _(pe):
            def mm(dst, lhsT, rhs, start=True, stop=True):
                return nc.tensor.matmul(dst, lhsT, rhs, start=start, stop=stop)

            def turn(dst, src, rows_=P):
                return nc.tensor.transpose(dst, src, ident[0:rows_, 0:rows_])

            pe.wait_ge(s["consts_ready"], 1)
            pe.wait_ge(s["rows_ready"], 1)
            turn(bank[7][:, 0:40], rows[:, :], 40).then_inc(s["cols_ready"], 1)
            pe.wait_ge(s["cols_copied"], 1)
            for n in range(ADA_UNITS):
                pe.wait_ge(landed[n % RING], 16 * (n // RING + 1))
                for kc in range(KC):
                    ins = mm(bank[n // 2][0:2, (n % 2) * 256:(n % 2) * 256 + 256], cols[:, kc:kc + 9:8],
                             wide(raw[n % RING])[:, kc, :], kc == 0, kc == KC - 1)
                ins.then_inc(s["ada_used"], 1)
                if n == 5:
                    pe.wait_ge(s["landed_conv"], 16)
                    turn(bank[7][:, 64:184], conv_rows[:, :], 120).then_inc(s["conv_turned"], 1)
            pe.wait_ge(s["ada_row_copied"], 4)
            for m in range(2 * KC):
                ins = turn(bank[4][:, 2 * m:2 * m + 2], ada_row[:, m * P:(m + 1) * P], 2)
            ins.then_inc(s["ada_turned"], 1)
            for kc in range(KC):
                if kc == 0:
                    pe.wait_ge(s["x_normed"], TILES)
                if kc >= 2:
                    pe.wait_ge(s["h_affine"], kc - 1)
                for t in range(TILES):
                    ins = turn(bank[5 + kc % 2][:, t * P:(t + 1) * P], x_nat[:, t, kc * P:(kc + 1) * P])
                ins.then_inc(s["xT_ready"], 1)
            pe.wait_ge(s["ab_split"], 1)
            pe.wait_ge(s["h_split"], KC)
            for t in range(TILES):
                for kc in range(KC):
                    dst, cols_t = bank[4][:, 32 * t:32 * t + 32], slice(t * P, (t + 1) * P)
                    mm(dst, hT_hi[:, kc, cols_t], ab_hi[:, kc, :], kc == 0, False)
                    mm(dst, hT_hi[:, kc, cols_t], ab_lo[:, kc, :], False, False)
                    ins = mm(dst, hT_lo[:, kc, cols_t], ab_hi[:, kc, :], False, kc == KC - 1)
            ins.then_inc(s["ab_sum"], 1)
            pe.wait_ge(s["gate_dve"], 2)
            for d in range(DIRS):
                mm(bank[5][:, 32 * d:32 * d + 32], causal[:, d, :],
                   gates[:, LOG_DECAY, :, :, :].rearrange("p t h d -> p (t h) d")[:, :, d])
            mm(bank[5][:, 64:128], ones[:, :], gates[:, LOG_DECAY, :, :, :].rearrange("p t h d -> p (t h d)"))\
                .then_inc(s["gate_sum"], 1)

            with pe.Fori(0, PAIRS) as i:
                pe.wait_ge(s["pair_free"], i + 1)

                def channels_first(j):
                    w0 = 0 if j < 2 else CTX
                    pe.wait_ge(s["unit_split"], i * 4 + (j + 1))
                    if j == 2:
                        pe.wait_ge(s["taps_done"], i * 6 + 2)
                    for ct in range(2):
                        dst = bank[(2 * j + ct) % 4][:, 0:TILES * P - w0]
                        for kc in range(KC):
                            hi = wide(w_hi[j % 2])[:, kc, ct * P:(ct + 1) * P]
                            lo = wide(w_lo[j % 2])[:, kc, ct * P:(ct + 1) * P]
                            mm(dst, hi, hT_hi[:, kc, w0:], kc == 0, False)
                            mm(dst, hi, hT_lo[:, kc, w0:], False, False)
                            ins = mm(dst, lo, hT_hi[:, kc, w0:], False, kc == KC - 1)
                        if ct == 0:
                            ins.then_inc(s["proj_ready"], 1)
                    ins.then_inc(s["proj_ready"], 1)

                def tokens_first(j):
                    pe.wait_ge(s["unit_split"], i * 4 + (j + 1))
                    pe.wait_ge(s["taps_done"], i * 6 + 4)
                    for t in range(2):
                        dst = bank[2 + t][:, 0:256]
                        tok = slice((LAT + t) * P, (LAT + t + 1) * P)
                        for kc in range(KC):
                            hi, lo = wide(w_hi[j % 2])[:, kc, :], wide(w_lo[j % 2])[:, kc, :]
                            mm(dst, hT_hi[:, kc, tok], hi, kc == 0, False)
                            mm(dst, hT_hi[:, kc, tok], lo, False, False)
                            ins = mm(dst, hT_lo[:, kc, tok], hi, False, kc == KC - 1)
                        ins.then_inc(s["proj_ready"], 1)

                def turn_channels(n):
                    tiles = TILES if n < 4 else 2
                    pe.wait_ge(s["chan_ready"], i * 6 + (n + 1))
                    if n == 2:
                        pe.wait_ge(s["k_normed"], i * 4 + 1)
                    if n == 3:
                        pe.wait_ge(s["k_normed"], i * 4 + 2)
                    if n >= 4:
                        pe.wait_ge(s["v_copied"], i * 2 + (n - 3))
                    for t in range(tiles):
                        ins = turn(bank[4 + n % 2][:, t * P:(t + 1) * P], chan[n][:, t * P:(t + 1) * P])
                    ins.then_inc(s["chan_turned"], 1)

                def turn_back(n, key):
                    pe.wait_ge(s["k_normed"], i * 4 + (key + 1))
                    if key >= 2:
                        pe.wait_ge(s["back_copied"], i * 4 + (key - 1))
                    for t in range(TILES if n < 4 else 2):
                        src = k_nat[:, n, t, :] if n < 4 else chan[n - 4][:, t * P:(t + 1) * P]
                        ins = turn(bank[6 + key % 2][:, t * P:(t + 1) * P], src)
                    ins.then_inc(s["back_turned"], 1)

                channels_first(0)
                channels_first(1)
                turn_channels(0)
                turn_channels(1)
                channels_first(2)
                turn_channels(2)
                turn_channels(3)
                turn_back(0, 0)
                turn_back(1, 1)
                tokens_first(3)
                turn_channels(4)
                turn_channels(5)
                turn_back(4, 2)
                turn_back(5, 3)

                for g in range(TILES):
                    if g == 0:
                        pe.wait_ge(s["back_copied"], i * 4 + 4)
                        pe.wait_ge(s["pair_ready"], i + 1)
                    if g >= 2:
                        pe.wait_ge(s["t_first"], i * 4 + (g - 1))
                    tok = slice(g * P, (g + 1) * P)
                    for h in range(2):
                        mm(bank[4 + g % 2][:, h * P:(h + 1) * P], kT[:, h, tok], kT[:, h, tok])
                        if g >= LAT:
                            q_tok = slice((g - LAT) * P, (g - LAT + 1) * P)
                            mm(bank[4 + g % 2][:, 256 + h * P:256 + (h + 1) * P], kT[:, h, tok], qT[:, h, q_tok])
                    for h in range(2):
                        for d in range(DIRS):
                            ins = mm(by_pair(bank[6 + g % 2])[:, h, d, :],
                                     pair_gates[:, LOG_DECAY, g, h, d:d + 1].to_broadcast([P, P]), causal[:, d, :])
                    ins.then_inc(s["scores_ready"], 1)
                for g in range(TILES):
                    pe.wait_ge(s["t_first"], i * 4 + (g + 1))
                    if g == 0:
                        pe.wait_ge(s["t_first"], i * 4 + 3)
                    if g == 1:
                        pe.wait_ge(s["t_first"], i * 4 + 4)
                    for h in range(2):
                        for d in range(DIRS):
                            ins = turn(by_pair(bank[4 + g])[:, h, d, :], t_inv[g][:, h, d, :])
                    ins.then_inc(s["u_turned"], 1)
                for l in range(N_LEVELS):
                    for g in range(TILES):
                        if l == 0:
                            pe.wait_ge(s["u_copied"], i * 4 + (g + 1))
                        else:
                            pe.wait_ge(s["t_copied"], i * 20 + (4 * l - 4 + g + 1))
                        for h in range(2):
                            for d in range(DIRS):
                                ins = mm(by_pair(bank[4 + g])[:, h, d, :], m_nat[g][:, h, d, :], u_inv[g][:, h, d, :])
                        ins.then_inc(s["p_sum"], 1)
                    for g in range(TILES):
                        pe.wait_ge(s["p_masked"], i * 24 + (4 * l + g + 1))
                        for h in range(2):
                            for d in range(DIRS):
                                ins = mm(by_pair(bank[4 + g])[:, h, d, :], t_inv[g][:, h, d, :], p_blk[g][:, h, d, :])
                        ins.then_inc(s["up_sum"], 1)
                    if l < N_LEVELS - 1:
                        for g in range(TILES):
                            pe.wait_ge(s["u_updated"], i * 24 + (4 * l + g + 1))
                            for h in range(2):
                                for d in range(DIRS):
                                    ins = turn(by_pair(bank[4 + g])[:, h, d, :], u_inv[g][:, h, d, :])
                            ins.then_inc(s["t_turned"], 1)
                pe.wait_ge(s["u_updated"], i * 24 + 24)
                for pos in range(TILES):
                    if pos:
                        pe.wait_ge(s["s_ready"], i * 3 + pos)
                        for h in range(2):
                            for d in range(DIRS):
                                t = chunk_at(pos, d)
                                ins = mm(by_pair(bank[4])[:, h, d, :], kT[:, h, t * P:(t + 1) * P], state[:, h, d, :])
                        ins.then_inc(s["ks_sum"], 1)
                    if pos >= LAT:
                        if pos > LAT:
                            pe.wait_ge(s["o_part"], i * 2 + (pos - LAT))
                        for h in range(2):
                            for d in range(DIRS):
                                t = chunk_at(pos, d) - LAT
                                ins = mm(by_pair(bank[6])[:, h, d, :], qT[:, h, t * P:(t + 1) * P], state[:, h, d, :])
                        ins.then_inc(s["qs_sum"], 1)
                    if pos:
                        pe.wait_ge(s["r_ready"], i * 3 + pos)
                    else:
                        pe.wait_ge(s["step_ready"], i * 4 + 1)
                    for h in range(2):
                        for d in range(DIRS):
                            rhs = r_val[:, h, d, :] if pos else v_beta[0][:, h, d, :]
                            ins = mm(by_pair(bank[5])[:, h, d, :], u_inv[chunk_at(pos, d)][:, h, d, :], rhs)
                    ins.then_inc(s["vnew_sum"], 1)
                    pe.wait_ge(s["vnew_copied"], i * 4 + (pos + 1))
                    if pos < TILES - 1:
                        for h in range(2):
                            for d in range(DIRS):
                                ins = mm(by_pair(bank[4])[:, h, d, :], k_dec[pos % 2][:, h, d, :], v_new[:, h, d, :])
                        ins.then_inc(s["s_sum"], 1)
                    if pos >= LAT:
                        for h in range(2):
                            for d in range(DIRS):
                                ins = mm(by_pair(bank[7])[:, h, d, :], intra[chunk_at(pos, d) - LAT][:, h, d, :],
                                         v_new[:, h, d, :])
                        ins.then_inc(s["intra_sum"], 1)

            def merge_unit(u, hi_src, lo_src, at, tiles):
                chunk, kh = u // 2, u % 2
                if kh == 0 and chunk >= 2:
                    if chunk - 2 < PB:
                        pe.wait_ge(s["drained_act"], chunk - 1)
                    else:
                        pe.wait_ge(s["drained_dve"], chunk - 1 - PB)
                pe.wait_ge(s["unit_split"], LOOP_UNITS + u + 1)
                for t in range(tiles):
                    dst = bank[2 * (chunk % 2) + t][:, :]
                    tok = slice(at + t * P, at + (t + 1) * P)
                    for kc in range(4):
                        k = 4 * kh + kc
                        hi, lo = four(w_hi[u % 2])[:, kc, :], four(w_lo[u % 2])[:, kc, :]
                        mm(dst, hi_src[:, k, tok], hi, k == 0, False)
                        mm(dst, hi_src[:, k, tok], lo, False, False)
                        ins = mm(dst, lo_src[:, k, tok], hi, False, k == KC - 1)
                ins.then_inc(s["unit_used"], 1)

            def turn_tokens(src):
                for b in range(4):
                    for kc in range(2):
                        for t in range(2):
                            ins = turn(bank[4 + b][:, kc * 256 + t * P:kc * 256 + (t + 1) * P], src(t, 2 * b + kc))
                    ins.then_inc(s["turned"], 1)

            pe.wait_ge(s["pair_free"], PAIRS + 1)
            pe.wait_ge(s["landed_mix"], 32)
            for b in range(2):
                for g in range(4):
                    ins = turn(bank[4 + b][:, g * P:(g + 1) * P], mix_raw[:, 4 * b + g, :])
                ins.then_inc(s["mix_turned"], 1)
            turn(bank[6][:, 0:8], rows[0:8, :], 8).then_inc(s["bias_turned"], 1)
            for u in range(8):
                merge_unit(u, hT_hi, hT_lo, CTX, 2)
            pe.wait_ge(s["o_gated"], 1)
            pe.wait_ge(s["mix_copied"], 3)
            turn_tokens(lambda t, k: o_nat[:, t, k, :])
            for u in range(8, 16):
                merge_unit(u, hT_hi, hT_lo, CTX, 2)
            pe.wait_ge(s["v_normed"], 1)
            pe.wait_ge(s["turned_lo"], 4)
            for t in range(2):
                for g in range(HEADS):
                    ins = mm(bank[4 + 2 * t + g // 4][:, (g % 4) * P:(g % 4 + 1) * P], mix_T[:, g, :],
                             v_act[:, t, g * P:(g + 1) * P])
                ins.then_inc(s["mix_sum"], 1)
            for u in range(2 * PB, 2 * PB + 2):
                merge_unit(u, hT_hi, hT_lo, 0, 2)
            pe.wait_ge(s["sgu_ready"], 1)
            turn_tokens(lambda t, k: u_act[:, t, k * P:(k + 1) * P])
            for u in range(2 * PB + 2, 2 * PA):
                merge_unit(u, hT_hi, hT_lo, 0, 2)
            pe.wait_ge(s["turned_lo"], 8)
            for u in range(2 * PA, 2 * ADA):
                merge_unit(u, hT_hi, hT_lo, 256, 2)
            pe.wait_ge(s["cond_split"], 2)
            for u in range(2 * ADA, 2 * ADA + 2):
                merge_unit(u, cond_hi, cond_lo, 0, 1)
            pe.wait_ge(s["merge_ready"], 1)
            turn_tokens(lambda t, k: merged[:, t, k * P:(k + 1) * P])
            for u in range(2 * ADA + 2, 2 * WO):
                merge_unit(u, cond_hi, cond_lo, 0, 1)
            pe.wait_ge(s["turned_lo"], 12)
            for u in range(2 * WO, MERGE_UNITS):
                merge_unit(u, hT_hi, hT_lo, 0, 2)
            pe.wait_ge(s["h2_ready"], 1)
            turn_tokens(lambda t, k: h2[:, t, k * P:(k + 1) * P])
            pe.wait_ge(s["turned_lo"], 16)
            for t in range(2):
                dst, tok = bank[0][:, EXPERTS * t:EXPERTS * (t + 1)], slice(256 + t * P, 256 + (t + 1) * P)
                for kc in range(KC):
                    mm(dst, hT_hi[:, kc, tok], router_hi[:, kc, :], kc == 0, False)
                    mm(dst, hT_hi[:, kc, tok], router_lo[:, kc, :], False, False)
                    ins = mm(dst, hT_lo[:, kc, tok], router_hi[:, kc, :], False, kc == KC - 1)
            ins.then_inc(s["logits_sum"], 1)
            pe.wait_ge(s["chosen_ready"], 1)
            mm(bank[0][:, 32:48], causal[:, 0, :], chosen[:, 0, :])
            mm(bank[0][:, 48:64], causal[:, 0, :], chosen[:, 1, :], True, False)
            mm(bank[0][:, 48:64], ones[:, :], chosen[:, 0, :], False, True)
            mm(bank[0][:, 64:80], ones[:, :], chosen[:, 0, :], True, False)
            mm(bank[0][:, 64:80], ones[:, :], chosen[:, 1, :], False, True).then_inc(s["counts_sum"], 1)
            pe.wait_ge(s["overflow_ready"], 1)
            for b in range(4):
                mm(bank[b][:, :], zero_bf[:, 0:P], zero_bf[:, :], True, False)
            pe.wait_ge(s["h2_split"], 1)

            def expert_turn(i, base):
                def at(n, per):
                    return i * per + (base * per + n)

                def split(k):
                    pe.wait_ge(s["unit_split"], i * PER_TURN + (LOOP_UNITS + MERGE_UNITS + base * PER_TURN + k + 1))

                def gather(g):
                    pe.wait_ge(s["picks_ready"], at(g + 1, 2))
                    for e in range(2):
                        for t in range(2):
                            turn(bank[6][:, e * 256 + t * P:e * 256 + (t + 1) * P], pick[g][:, t, e, :].bitcast(F32))
                    for e in range(2):
                        for t in range(2):
                            ins = mm(bank[7][:, e:e + 1], pick[g][:, t, e, :].bitcast(F32),
                                     choice[:, t, bass.ds(i * 4 + (2 * g + e), 1)], t == 0, t == 1)
                    ins.then_inc(s["spread_sum"], 1)
                    for c in range(4):
                        if c < 2:
                            pe.wait_ge(s["gathered_lo"], at(5 * g + 1, 10))
                        else:
                            pe.wait_ge(s["gathered_lo"], at(5 * g + c, 10))
                        for kc in range(2):
                            dst = bank[6 + (c + 1) % 2][:, kc * 256:kc * 256 + 256]
                            ch = slice((2 * c + kc) * P, (2 * c + kc + 1) * P)
                            for t in range(2):
                                rhs = pick[g][:, t, :, :].rearrange("p e n -> p (e n)")
                                mm(dst, h2_hi[:, t, ch], rhs, t == 0, False)
                                ins = mm(dst, h2_lo[:, t, ch], rhs, False, t == 1)
                        ins.then_inc(s["gathered"], 1)

                def up(q):
                    for m in range(2):
                        dst = bank[4 + (q + m) % 2][:, :]
                        if m == 0:
                            pe.wait_ge(s["gathered_lo"], at(5 * (q // 2) + 5, 10))
                        elif q:
                            pe.wait_ge(s["act_split"], at(q, 4))
                        for kh in range(2):
                            k = UP_AT[q] + 2 * m + kh
                            split(k)
                            for kc in range(4):
                                c = 4 * kh + kc
                                tok = slice(256 * (q // 2) + P * (q % 2), 256 * (q // 2) + P * (q % 2) + P)
                                hi, lo = four(e_hi[k % 3])[:, kc, :], four(e_lo[k % 3])[:, kc, :]
                                mm(dst, hT_hi[:, c, tok], hi, c == 0, False)
                                mm(dst, hT_hi[:, c, tok], lo, False, False)
                                ins = mm(dst, hT_lo[:, c, tok], hi, False, c == KC - 1)
                            ins.then_inc(s["unit_used"], 1)

                def turn_act(q):
                    pe.wait_ge(s["act_done"], at(q + 1, 4))
                    for c in range(4):
                        ins = turn(bank[4 + q % 2][:, c * P:(c + 1) * P], act_nat[:, c * P:(c + 1) * P])
                    ins.then_inc(s["act_turned"], 1)

                def down(q):
                    pe.wait_ge(s["act_split"], at(q + 1, 4))
                    for nh in range(2):
                        k = DOWN_AT[q] + nh
                        split(k)
                        for c in range(4):
                            hi, lo = four(e_hi[k % 3])[:, c, :], four(e_lo[k % 3])[:, c, :]
                            mm(bank[7 - nh][:, :], act_hi[:, c, :], hi, c == 0, False)
                            mm(bank[7 - nh][:, :], act_hi[:, c, :], lo, False, False)
                            ins = mm(bank[7 - nh][:, :], act_lo[:, c, :], hi, False, c == 3)
                        ins.then_inc(s["unit_used"], 1)

                def scatter(q):
                    pe.wait_ge(s["spread_copied"], at(q // 2 + 1, 2))
                    pe.wait_ge(s["y_split"], at(2 * q + 2, 8))
                    for t in range(2):
                        to = spread[q // 2][:, q % 2, t * P:(t + 1) * P]
                        for nh in range(2):
                            mm(bank[2 * t + nh][:, :], to, y_hi[:, nh * N:nh * N + N], False, False)
                            ins = mm(bank[2 * t + nh][:, :], to, y_lo[:, nh * N:nh * N + N], False, False)
                    ins.then_inc(s["scattered"], 1)

                gather(0)
                up(0)
                gather(1)
                turn_act(0)
                up(1)
                down(0)
                turn_act(1)
                scatter(0)
                up(2)
                down(1)
                turn_act(2)
                scatter(1)
                up(3)
                down(2)
                turn_act(3)
                scatter(2)
                down(3)
                scatter(3)

            with pe.Fori(0, TURNS) as i:
                expert_turn(i, 0)
            with pe.If(pe.value_load(overflow_int[0:1, 0:1], min_val=0, max_val=1) > 0):
                with pe.Fori(0, TURNS) as i:
                    expert_turn(i, TURNS)
            for b in range(4):
                ins = mm(bank[b][:, :], zero_bf[:, 0:P], zero_bf[:, :], False, True)
            ins.then_inc(s["sum_closed"], 1)


_INS = ['x', 'c', 'ctx', 'c_ctx', 'w_ada', 'b_ada', 'norm1_g', 'norm2_g', 'w_in', 'a_ln_g', 'a_w_s', 'a_b_s',
        'b_conv_w', 'b_A_log', 'b_dt_bias', 'b_norm_g', 'w_proj_a', 'w_proj_b', 'w_out',
        'w_router', 'b_router', 'w_e1', 'w_e3', 'w_e2', 'final_g']
_OUT = ((1, SEQ, D), 'float32')


def kernel(**inputs):
    import numpy as np
    import concourse.bacc as bacc
    from concourse.bass_utils import run_bass_kernel_spmd

    nc = bacc.Bacc("TRN2", target_bir_lowering=False, num_devices=1)
    arrays, args = {}, []
    for name in _INS:
        a = np.ascontiguousarray(inputs[name])
        arrays[f"in_{name}_dram"] = a
        args.append(nc.dram_tensor(f"in_{name}_dram", a.shape, mybir.dt.from_np(a.dtype), kind="ExternalInput").ap())
    shape, dtype = _OUT
    args.append(nc.dram_tensor("out_0_dram", shape, mybir.dt.from_np(np.dtype(dtype)), kind="ExternalOutput").ap())
    block_kernel(nc, *args)
    r = run_bass_kernel_spmd(nc, [arrays], core_ids=[0])
    return r.results[0]["out_0_dram"]
```
